# Optimizing a Trainium2 kernel written in Bass

```python
import jax, jax.numpy as jnp
from jax import lax
import numpy as np

D_MODEL = 1024
BATCH = 1
SEQ = 256
DEPTH = 2

HEAD_DIM = 64
A_Q_HEADS = 8
A_KV_HEADS = 2
B_GROUP_CFG = ((128, 1), (512, 4), (2048, 16))
B_HEADS_PER_GROUP = 4
B_GROUPS = len(B_GROUP_CFG)
B_HEADS = B_GROUPS * B_HEADS_PER_GROUP
POOL_WINDOWS = (2, 4, 8, 16)
POOL_GROUPS = len(POOL_WINDOWS)
POOL_GROUP_WIDTH = 128
POOL_WIDTH = POOL_GROUPS * POOL_GROUP_WIDTH
N_BRANCHES = 3
D_FF = ((-(-8 * D_MODEL // 3) + 255) // 256) * 256
GRID_W = 64
ROPE_THETA = 10000.0
BLOCK = 128
EPS = 1e-6
NEG_INF = -1e30

A_Q_WIDTH = A_Q_HEADS * HEAD_DIM
A_KV_WIDTH = A_KV_HEADS * HEAD_DIM
B_WIDTH = B_HEADS * HEAD_DIM
B_OUT_WIDTH = B_HEADS_PER_GROUP * HEAD_DIM
GATE_WIDTH = N_BRANCHES * D_MODEL
IN_WIDTH = A_Q_WIDTH + 2 * A_KV_WIDTH + 3 * B_WIDTH + POOL_WIDTH + GATE_WIDTH
SPLIT_POINTS = (
    A_Q_WIDTH,
    A_Q_WIDTH + A_KV_WIDTH,
    A_Q_WIDTH + 2 * A_KV_WIDTH,
    A_Q_WIDTH + 2 * A_KV_WIDTH + B_WIDTH,
    A_Q_WIDTH + 2 * A_KV_WIDTH + 2 * B_WIDTH,
    A_Q_WIDTH + 2 * A_KV_WIDTH + 3 * B_WIDTH,
    A_Q_WIDTH + 2 * A_KV_WIDTH + 3 * B_WIDTH + POOL_WIDTH,
)
RESID_SCALE = (2 * DEPTH) ** -0.5

kernel_name = 'hybrid_gated_axial_dilated_pool_encoder'

def rms_norm(x, g):
    xf = x.astype(jnp.float32)
    y = xf * lax.rsqrt(jnp.mean(xf * xf, axis=-1, keepdims=True) + EPS)
    return (y * g.astype(jnp.float32)).astype(x.dtype)

def rope_angles(pos, dim):
    inv = ROPE_THETA ** (-jnp.arange(0, dim, 2, dtype=jnp.float32) / dim)
    return pos.astype(jnp.float32)[:, None] * inv[None, :]

def apply_rope(x, ang):
    xf = x.astype(jnp.float32)
    x1, x2 = jnp.split(xf, 2, axis=-1)
    c = jnp.cos(ang)[None, :, None, :]
    s = jnp.sin(ang)[None, :, None, :]
    return jnp.concatenate([x1 * c - x2 * s, x2 * c + x1 * s], axis=-1).astype(x.dtype)

def apply_axial_rope(x, ang_row, ang_col):
    xr, xc = jnp.split(x, 2, axis=-1)
    return jnp.concatenate([apply_rope(xr, ang_row), apply_rope(xc, ang_col)], axis=-1)

def dense_gqa_blocked(q, k, v):
    b, s, hq, dh = q.shape
    hkv = k.shape[2]
    g = hq // hkv
    nb = s // BLOCK
    scale = dh ** -0.5
    qb = q.reshape(b, nb, BLOCK, hkv, g, dh).transpose(1, 0, 2, 3, 4, 5)

    def one_block(q_blk):
        sc = jnp.einsum('bqkgd,bskd->bkgqs', q_blk, k, preferred_element_type=jnp.float32) * scale
        p = jax.nn.softmax(sc, axis=-1)
        return jnp.einsum('bkgqs,bskd->bqkgd', p.astype(v.dtype), v)

    o = lax.map(one_block, qb)
    return o.transpose(1, 0, 2, 3, 4, 5).reshape(b, s, hq * dh)

def dilated_window_attention(q, k, v, dilation, half_span):
    b, s, h, dh = q.shape
    L = s // dilation
    nb = -(-L // BLOCK)
    lp = nb * BLOCK
    bd = b * dilation

    def to_sub(t):
        t = t.reshape(b, L, dilation, h, dh).transpose(0, 2, 1, 3, 4).reshape(bd, L, h, dh)
        return jnp.pad(t, ((0, 0), (0, lp - L), (0, 0), (0, 0)))

    def band(t):
        tp = jnp.pad(t, ((0, 0), (BLOCK, BLOCK), (0, 0), (0, 0)))
        return jnp.concatenate(
            [tp[:, i * BLOCK:i * BLOCK + lp].reshape(bd, nb, BLOCK, h, dh) for i in range(3)], axis=2)

    qb = to_sub(q).reshape(bd, nb, BLOCK, h, dh)
    kb = band(to_sub(k))
    vb = band(to_sub(v))
    sc = jnp.einsum('znqhd,znkhd->znhqk', qb, kb, preferred_element_type=jnp.float32) * (dh ** -0.5)
    blk = jnp.arange(nb)[:, None, None] * BLOCK
    qpos = blk + jnp.arange(BLOCK)[None, :, None]
    kpos = blk - BLOCK + jnp.arange(3 * BLOCK)[None, None, :]
    valid = (jnp.abs(qpos - kpos) <= half_span) & (kpos >= 0) & (kpos < L)
    sc = jnp.where(valid[None, :, None], sc, NEG_INF)
    m = jnp.max(sc, axis=-1, keepdims=True)
    p = jnp.exp(sc - m)
    den = jnp.sum(p, axis=-1, keepdims=True)
    o = jnp.einsum('znhqk,znkhd->znqhd', (p / den).astype(v.dtype), vb)
    lse = (m + jnp.log(den))[..., 0]
    o = o.reshape(b, dilation, lp, h, dh)[:, :, :L].transpose(0, 2, 1, 3, 4).reshape(b, s, h, dh)
    lse = lse.transpose(0, 1, 3, 2).reshape(b, dilation, lp, h)[:, :, :L]
    lse = lse.transpose(0, 2, 1, 3).reshape(b, s, h)
    return o, lse

def multiscale_pool(u, lin, scale):
    b, s, _ = u.shape
    uf = u.astype(jnp.float32).reshape(b, s, POOL_GROUPS, POOL_GROUP_WIDTH)
    cs = jnp.pad(lax.cumsum(uf, axis=1), ((0, 0), (1, 0), (0, 0), (0, 0)))
    t = jnp.arange(s)
    outs = []
    for gi, w in enumerate(POOL_WINDOWS):
        lo = jnp.clip(t - w // 2, 0, s)
        hi = jnp.clip(t + w - w // 2, 0, s)
        mean = (cs[:, hi, gi] - cs[:, lo, gi]) / (hi - lo).astype(jnp.float32)[None, :, None]
        outs.append(mean - uf[:, :, gi])
    pooled = jnp.stack(outs, axis=2).astype(u.dtype)
    mixed = jnp.einsum('bsgc,gcd->bsgd', pooled, lin)
    return mixed.reshape(b, s, POOL_WIDTH) * scale

def setup_inputs(seed: int = 0) -> dict:
    key = jax.random.key(seed)
    ks = jax.random.split(key, 19)
    f32 = jnp.float32

    def nrm(k, shape, fan_in):
        return jax.random.normal(k, shape, f32) * (fan_in ** -0.5)

    def gain(k, shape):
        return 1.0 + 0.02 * jax.random.normal(k, shape, f32)

    return {
        'x': jax.random.normal(ks[0], (BATCH, SEQ, D_MODEL), f32),
        'norm_mix': gain(ks[1], (DEPTH, D_MODEL)),
        'w_in': nrm(ks[2], (DEPTH, D_MODEL, IN_WIDTH), D_MODEL),
        'b_gate': 0.02 * jax.random.normal(ks[3], (DEPTH, GATE_WIDTH), f32),
        'qn_a': gain(ks[4], (DEPTH, HEAD_DIM)),
        'kn_a': gain(ks[5], (DEPTH, HEAD_DIM)),
        'qn_b': gain(ks[6], (DEPTH, HEAD_DIM)),
        'kn_b': gain(ks[7], (DEPTH, HEAD_DIM)),
        'pool_lin': nrm(ks[8], (DEPTH, POOL_GROUPS, POOL_GROUP_WIDTH, POOL_GROUP_WIDTH), POOL_GROUP_WIDTH),
        'pool_scale': gain(ks[9], (DEPTH, POOL_WIDTH)),
        'w_branch_a': nrm(ks[10], (DEPTH, A_Q_WIDTH, D_MODEL), A_Q_WIDTH),
        'w_branch_b': nrm(ks[11], (DEPTH, B_OUT_WIDTH, D_MODEL), B_OUT_WIDTH),
        'w_branch_c': nrm(ks[12], (DEPTH, POOL_WIDTH, D_MODEL), POOL_WIDTH),
        'w_out': nrm(ks[13], (DEPTH, D_MODEL, D_MODEL), D_MODEL) * RESID_SCALE,
        'norm_ffn': gain(ks[14], (DEPTH, D_MODEL)),
        'w_ffn_gate': nrm(ks[15], (DEPTH, D_MODEL, D_FF), D_MODEL),
        'w_ffn_up': nrm(ks[16], (DEPTH, D_MODEL, D_FF), D_MODEL),
        'w_ffn_down': nrm(ks[17], (DEPTH, D_FF, D_MODEL), D_FF) * RESID_SCALE,
    }

def reference(x, norm_mix, w_in, b_gate, qn_a, kn_a, qn_b, kn_b, pool_lin, pool_scale,
              w_branch_a, w_branch_b, w_branch_c, w_out, norm_ffn, w_ffn_gate, w_ffn_up, w_ffn_down):
    b, s, _ = x.shape
    rows = s // GRID_W
    row_idx = jnp.repeat(jnp.arange(rows), GRID_W)
    col_idx = jnp.tile(jnp.arange(GRID_W), rows)
    ang_row = rope_angles(row_idx, HEAD_DIM // 2)
    ang_col = rope_angles(col_idx, HEAD_DIM // 2)
    ang_seq = rope_angles(jnp.arange(s), HEAD_DIM)

    for l in range(DEPTH):
        h = rms_norm(x, norm_mix[l])
        z = h @ w_in[l]
        qa, ka, va, qb, kb, vb, uc, gz = jnp.split(z, SPLIT_POINTS, axis=-1)

        qa = apply_axial_rope(rms_norm(qa.reshape(b, s, A_Q_HEADS, HEAD_DIM), qn_a[l]), ang_row, ang_col)
        ka = apply_axial_rope(rms_norm(ka.reshape(b, s, A_KV_HEADS, HEAD_DIM), kn_a[l]), ang_row, ang_col)
        va = va.reshape(b, s, A_KV_HEADS, HEAD_DIM)
        ya = dense_gqa_blocked(qa, ka, va) @ w_branch_a[l]

        qb = apply_rope(rms_norm(qb.reshape(b, s, B_HEADS, HEAD_DIM), qn_b[l]), ang_seq)
        kb = apply_rope(rms_norm(kb.reshape(b, s, B_HEADS, HEAD_DIM), kn_b[l]), ang_seq)
        qb = qb.reshape(b, s, B_GROUPS, B_HEADS_PER_GROUP, HEAD_DIM)
        kb = kb.reshape(b, s, B_GROUPS, B_HEADS_PER_GROUP, HEAD_DIM)
        vb = vb.reshape(b, s, B_GROUPS, B_HEADS_PER_GROUP, HEAD_DIM)
        o_list, lse_list = [], []
        for gi, (window, dil) in enumerate(B_GROUP_CFG):
            o_g, lse_g = dilated_window_attention(qb[:, :, gi], kb[:, :, gi], vb[:, :, gi], dil, window // (2 * dil))
            o_list.append(o_g)
            lse_list.append(lse_g)
        wts = jax.nn.softmax(jnp.stack(lse_list, axis=0), axis=0)
        ob = jnp.einsum('gbsh,gbshd->bshd', wts.astype(x.dtype), jnp.stack(o_list, axis=0))
        yb = ob.reshape(b, s, B_OUT_WIDTH) @ w_branch_b[l]

        yc = multiscale_pool(uc, pool_lin[l], pool_scale[l]) @ w_branch_c[l]

        gates = jax.nn.sigmoid(gz + b_gate[l]).reshape(b, s, N_BRANCHES, D_MODEL)
        merged = gates[:, :, 0] * ya + gates[:, :, 1] * yb + gates[:, :, 2] * yc
        x = x + merged @ w_out[l]

        h2 = rms_norm(x, norm_ffn[l])
        x = x + (jax.nn.silu(h2 @ w_ffn_gate[l]) * (h2 @ w_ffn_up[l])) @ w_ffn_down[l]
    return x


_drawn_inputs = setup_inputs


def setup_inputs(seed=0):
    import zlib

    import numpy as np

    out = dict(_drawn_inputs(seed))
    spreads = {}
    factors = {'norm_mix': 7.331,
     'b_gate': 8.0,
     'qn_a': 8.0,
     'kn_a': 8.0,
     'qn_b': 8.0,
     'kn_b': 8.0,
     'pool_scale': 8.0,
     'norm_ffn': 4.945}
    for name, (base, spread) in spreads.items():
        noise = np.random.default_rng([zlib.crc32(name.encode()), seed]).standard_normal(out[name].shape)
        drawn = base * np.exp(spread * noise) if base else spread * noise
        out[name] = __import__('jax').numpy.asarray(drawn.astype(out[name].dtype))
    for name, factor in factors.items():
        out[name] = (out[name] * factor).astype(out[name].dtype)
    return out
```

```python
from contextlib import ExitStack

import concourse.bass as bass
from concourse import mybir

F32 = mybir.dt.float32
F32R = mybir.dt.float32r
BF16 = mybir.dt.bfloat16
ALU = mybir.AluOpType
ACT = mybir.ActivationFunctionType
AX_X = mybir.AxisListType.X

P = 128
DEPTH, SEQ, D = 2, 256, 1024
HD = 64
EPS = 1e-6
NEG_INF = -1e30
MT = SEQ // P
KT = D // P
NC = 512
UK = 4
UNIT = UK * NC
D_FF = 2816
A_Q, A_KV, B_W, POOL_W = 512, 128, 768, 512
GROUPS, SLOTS = 3, 4
POOL_G = 4
Z_CHUNKS, GATE_CHUNK, POOL_CHUNK = 13, 7, 6
FC = D_FF // 256
KF = D_FF // P
RING = 4

U_Z = 0
U_C0, U_C1, U_A0, U_B, U_A1 = 26, 27, 28, 29, 30
U_OUT = 31
U_FFN = 35
U_DOWN = U_FFN + 2 * FC
UNITS = U_DOWN + 11
assert UNITS % RING == 0

QK_A_Q, QK_A_K, QK_B_Q, QK_B_K = 0, 512, 640, 1408
QK_W = 2176
VU_A, VU_B, VU_POOL = 0, 128, 896
VU_W = 1408
Z_PIECES = [
    [(0, 512, "qk", 0)],
    [(0, 128, "qk", 512), (128, 128, "vu", 0), (256, 256, "qk", 640)],
    [(0, 512, "qk", 896)],
    [(0, 512, "qk", 1408)],
    [(0, 256, "qk", 1920), (256, 256, "vu", 128)],
    [(0, 512, "vu", 384)],
    [(0, 512, "vu", 896)],
]
REGIONS = [
    ("a_q", QK_A_Q, 8, 0, 0, 0, (2, 3)),
    ("a_k", QK_A_K, 2, 8, 1, 1, (4, 4)),
    ("b_q", QK_B_Q, 12, 10, 2, 2, (6, 7)),
    ("b_k", QK_B_K, 12, 22, 3, 4, (10, 11)),
]
HEADS = 34
QT_A_Q, QT_A_K, QT_B_Q, QT_B_K, QTILES = 0, 4, 5, 11, 17

PR_MIX, PR_FFN, PR_PS, PR_GAIN, PR_LIN = 0, 8, 16, 20, 20 + 4 * HD
PR_W = PR_LIN + POOL_G * P

ATT = 16
ATT_STEP = 10


def turn_batches(t):
    out = []
    if 0 <= t - ATT_STEP - 1 < ATT:
        out.append(("probs", t - ATT_STEP - 1))
    at = {
        0: [("mix_x", 0), ("mix_x", 1)], 1: [("mix_x", 2), ("mix_x", 3)],
        5: [("qk", 0)], 6: [("qk", 1)], 7: [("qk", 2)],
        9: [("qk", 3)], 10: [("qk", 4)], 11: [("qk", 5)],
        13: [("qk", 6)], 14: [("qk", 7), ("qk", 8)],
        17: [("pool", 0), ("pool", 1)], 20: [("mixed", 0), ("mixed", 1)],
        19: [("heads", 0)], 23: [("heads", 1)], 26: [("heads", 2)], 29: [("heads", 3)],
        31: [("merged", 0), ("merged", 1)], 33: [("merged", 2), ("merged", 3)],
        35: [("ffn_x", 0), ("ffn_x", 1)], 36: [("ffn_x", 2), ("ffn_x", 3)],
    }
    out += at.get(t, [])
    i, odd = divmod(t - U_FFN - 3, 2)
    if 0 <= i < FC and not odd:
        out.append(("hidden", i))
    return out


QK_BATCH = [(0, 2), (2, 2), (4, 1), (5, 2), (7, 2), (9, 2), (11, 2), (13, 2), (15, 2)]
SCALED = ("mix_x", "mixed", "ffn_x")
SPLIT = ("heads", "merged", "hidden")
PLAIN = ("qk", "probs", "pool")


def plan_banks():
    order = {b: [] for b in range(8)}

    def pair(first, name):
        for m in range(MT):
            order[first + m].append((name, m))

    for c in range(Z_CHUNKS):
        pair(2 if c in (0, 2, 4) else 0, f"z{c}")
    order[2] += [("o", 0), ("o", 2)]
    order[3] += [("o", 1), ("o", 3)]
    for i in range(ATT):
        order[4 + i % 2].append(("s", i))
    pair(4, "C1")
    pair(0, "C0")
    pair(0, "A0")
    pair(2, "B0")
    pair(4, "B1")
    pair(0, "A1")
    pair(4, "W0")
    pair(2, "W1")
    for i in range(FC):
        pair(2 * (i % 2), f"f{i}")
    pair(2, "D0")
    pair(0, "D1")
    n = 0
    for t in range(UNITS):
        for b in turn_batches(t):
            order[6 + n % 2].append(b)
            n += 1
    assert n % 2 == 0
    use = {name: (b, k) for b, names in order.items() for k, name in enumerate(names)}
    return order, use, {b: len(names) for b, names in order.items()}


ORDER, USE, USES = plan_banks()

UNIT_ENDS = {(f"z{c}", 1): 2 * c + 1 for c in range(Z_CHUNKS)}
UNIT_ENDS |= {("C0", 1): U_C0, ("C1", 1): U_C1, ("A0", 1): U_A0, ("B1", 1): U_B, ("A1", 1): U_A1,
              ("W0", 1): U_OUT + 2, ("W1", 1): U_OUT + 3, ("D1", 1): U_DOWN + 10}
UNIT_ENDS |= {(f"f{i}", 1): U_FFN + 2 * i + 1 for i in range(FC)}
FULL = {name: n for b in ORDER for n, name in enumerate([x for x in ORDER[b] if x not in UNIT_ENDS])}
FULLS = {b: len([x for x in names if x not in UNIT_ENDS]) for b, names in ORDER.items()}

HI_TURNS = [b for t in range(UNITS) for b in turn_batches(t) if b[0] in SCALED + SPLIT]
SCALED_TURNS = [b for b in HI_TURNS if b[0] in SCALED]
VECTOR_LINKS = 12 + 8 * 4 + 4 + 2 * MT + MT * FC
POOL_LINKS = 12


def splits_at(t):
    if t == 0:
        return [1]
    if t == 1:
        return [2, 3]
    return [t + 2] if t + 2 < UNITS else []


def build(nc, x, stream, params, b_gate, const, mask, out):
    stream_v = stream.rearrange("u p n -> (u p) n")
    params_v = params.rearrange("l p n -> (l p) n")
    gate_v = b_gate.rearrange("l g n -> (l g) n")
    with ExitStack() as ctx:
        def sb(name, shape, dt=F32, to=ctx):
            return to.enter_context(nc.sbuf_tensor(name, shape, dt))

        def sem(name):
            return ctx.enter_context(nc.semaphore(name))

        w_hi = sb("w_hi", [P, RING, UK, NC], F32R)
        with ExitStack() as shared:
            w_raw = sb("w_raw", [P, RING, UK, NC], F32, shared)
        w_lo = sb("w_lo", [P, RING, UK, NC], F32R)
        x_sb = sb("x_sb", [P, MT, D])
        aT_hi = sb("aT_hi", [P, KT, SEQ], F32R)
        aT_lo = sb("aT_lo", [P, KT, SEQ], F32R)
        qkT = sb("qkT", [P, QTILES, SEQ])
        probs = sb("probs", [P, 2, NC])
        probsT = sb("probsT", [P, 2, NC])
        scratch = sb("scratch", [P, 2 * B_W])
        bias_sb = sb("bias_sb", [P, 2, NC])
        con = sb("con", [P, P + 4 * MT * HD + MT * POOL_G * SEQ])
        mask_sb = sb("mask_sb", [P, P + MT * NC], BF16)
        rope = sb("rope", [P, 4, 2, MT, HD])
        par = sb("par", [P, PR_W])
        mixT_hi = sb("mixT_hi", [P, POOL_G, SEQ], F32R)
        mixT_lo = sb("mixT_lo", [P, POOL_G, SEQ], F32R)
        oT_hi = sb("oT_hi", [P, 6, SEQ], F32R)
        oT_lo = sb("oT_lo", [P, 6, SEQ], F32R)
        ss = sb("ss", [P, MT, HEADS])
        rs = sb("rs", [P, MT, HEADS])
        rs_in = sb("rs_in", [P, MT, HEADS])
        neg_half = sb("neg_half", [P, MT, HEADS])
        ssx = sb("ssx", [P, 2, MT])
        sx = sb("sx", [P, 2, MT])
        rstd = sb("rstd", [P, 2, MT])
        neg_max = sb("neg_max", [P, 2 * ATT])
        den = sb("den", [P, MT, 8 + SLOTS])
        rden = sb("rden", [P, MT, 8 + SLOTS])
        with ExitStack() as mixer:
            with ExitStack() as early:
                zqk = sb("zqk", [P, MT, QK_W], F32, early)
            with ExitStack() as late:
                heads = sb("heads", [P, MT, A_Q + SLOTS * HD], F32, late)
                merged = sb("merged", [P, MT, D], F32, late)
                pooledT = sb("pooledT", [P, POOL_G, SEQ], F32, late)
            sb("late_room", [P, MT * (A_Q + SLOTS * HD) + MT * D + POOL_G * SEQ], F32, mixer)
            zvu = sb("zvu", [P, MT, VU_W], F32, mixer)
            gates = sb("gates", [P, MT, 3 * D], F32, mixer)
        hT_hi = sb("hT_hi", [P, KF, SEQ], F32R)
        hT_lo = sb("hT_lo", [P, KF, SEQ], F32R)
        sg = sb("sg", [P, 2, MT, 256])
        hid = sb("hid", [P, 2, MT, 256])

        ident = con[:, 0:P]
        rope_const = con[:, P:P + 4 * MT * HD].rearrange("p (k m d) -> p k m d", k=4, m=MT)
        pool_mat = con[:, P + 4 * MT * HD:].rearrange("p (m g n) -> p m g n", m=MT, g=POOL_G)
        ident_b = mask_sb[:, 0:P]
        mask_m = [mask_sb[:, P + m * NC:P + (m + 1) * NC] for m in range(MT)]
        lin = par[:, PR_LIN:PR_W].rearrange("p (g d) -> p g d", g=POOL_G)
        gate_v3 = gates[:, :, :].rearrange("p m (b n c) -> p m b n c", b=3, n=2)

        bank = [ctx.enter_context(nc.psum_tensor(f"bank{b}", [P, NC], F32)) for b in range(8)]

        x_loaded = sem("x_loaded")
        const_loaded = sem("const_loaded")
        mask_loaded = sem("mask_loaded")
        mask_ready = sem("mask_ready")
        params_loaded = sem("params_loaded")
        bias_loaded = [sem(f"bias_loaded{i}") for i in range(2)]
        unit_landed = [sem(f"unit_landed{i}") for i in range(RING)]
        unit_done = sem("unit_done")
        unit_hi = sem("unit_hi")
        unit_lo = sem("unit_lo")
        bank_full = [sem(f"bank_full{b}") for b in range(8)]
        bank_free = [sem(f"bank_free{b}") for b in range(8)]
        scaled = sem("scaled")
        turn_hi = sem("turn_hi")
        turn_lo = sem("turn_lo")
        half_ready = sem("half_ready")
        head_sums = sem("head_sums")
        head_norms = sem("head_norms")
        rotated = sem("rotated")
        x_sums = sem("x_sums")
        x_norm = sem("x_norm")
        max_ready = sem("max_ready")
        exp_done = sem("exp_done")
        gate_done = sem("gate_done")
        merged_ready = sem("merged_ready")
        sig_done = sem("sig_done")
        vchain = sem("vchain")
        pchain = sem("pchain")
        out_done = sem("out_done")

        def B(name):
            return bank[USE[name][0]]

        def wait_free(eng, lay, name):
            b, k = USE[name]
            eng.wait_ge(bank_free[b], lay * USES[b] + (k + 1))

        def wait_full(eng, lay, name):
            if name in UNIT_ENDS:
                eng.wait_ge(unit_done, lay * UNITS + (RING + UNIT_ENDS[name] + 1))
            else:
                b = USE[name][0]
                eng.wait_ge(bank_full[b], lay * FULLS[b] + (FULL[name] + 1))

        def wait_emptied(eng, lay, name):
            b, k = USE[name]
            eng.wait_ge(bank_free[b], lay * USES[b] + (k + 2))

        def full(ins, name):
            if name not in UNIT_ENDS:
                ins.then_inc(bank_full[USE[name][0]], 1)

        def free(ins, name):
            ins.then_inc(bank_free[USE[name][0]], 1)

        def turn_dest(name, hi):
            kind, i = name
            if kind in ("mix_x", "merged", "ffn_x"):
                to = aT_hi if hi else aT_lo
                return to[:, UK * (i // 2):UK * (i // 2) + UK, P * (i % 2):P * (i % 2) + P]
            if kind == "mixed":
                return (mixT_hi if hi else mixT_lo)[:, 2 * i:2 * i + 2, :]
            if kind == "heads":
                to, m = (oT_hi if hi else oT_lo), i % 2
                return to[:, 0:4, m * P:m * P + P] if i < 2 else to[:, 4:6, m * P:m * P + P]
            to = hT_hi if hi else hT_lo
            return to[:, 2 * i:2 * i + 2, :]

        def turn_view(name, ap):
            kind, i = name
            if kind in ("mix_x", "merged", "ffn_x"):
                return ap.rearrange("p (k n) -> p k n", k=UK)
            if kind == "heads":
                return ap.rearrange("p (k n) -> p k n", k=4) if i < 2 else \
                    ap[:, 0:2 * P].rearrange("p (k n) -> p k n", k=2)
            return ap.rearrange("p (k n) -> p k n", k=2)

        block = ctx.enter_context(nc.Block())

        @block.sync
        def _(sp):
            xv = x.rearrange("b (p m) d -> (b p) m d", m=MT)
            sp.dma_start(x_sb[:, :, :], xv).then_inc(x_loaded, 16)
            sp.dma_start(con[:, :], const).then_inc(const_loaded, 16)
            with sp.Fori(0, DEPTH * UNITS // RING) as turn:
                for s in range(RING):
                    sp.wait_ge(unit_done, turn * RING + (s + 1))
                    sp.dma_start(w_raw[:, s, :, :].rearrange("p k n -> p (k n)"),
                                 stream_v[bass.ds((turn * RING + s) * P, P), :]
                                 ).then_inc(unit_landed[s], 16)
            for b in range(4):
                sp.wait_ge(bank_free[b], DEPTH * USES[b] + 1)
            ov = out.rearrange("b (p m) d -> (b p) m d", m=MT)
            sp.dma_start(ov, x_sb[:, :, :]).then_inc(out_done, 16)
            sp.wait_ge(out_done, 16)

        @block.gpsimd
        def _(pool):
            pool.dma_start(gates[:, 0, 0:MT * NC], mask).then_inc(mask_loaded, 16)
            nc.gpsimd.memset(neg_half[:, :, :], -0.5).then_inc(half_ready, 1)
            pool.wait_ge(half_ready, 1)

            def power(lay, link, dst, src, mul, eps, signal):
                nc.gpsimd.tensor_scalar(dst[1], src, mul, eps, ALU.mult, ALU.add).then_inc(pchain, 1)
                pool.wait_ge(pchain, lay * POOL_LINKS + (link + 1))
                nc.gpsimd.tensor_tensor(dst[0], dst[1], dst[2], ALU.pow).then_inc(signal, 1)

            def x_norms(lay, which, link):
                pool.wait_ge(x_sums, lay * 8 + 4 * (which + 1))
                nc.gpsimd.tensor_tensor(sx[:, which, :], ssx[:, 0, :], ssx[:, 1, :], ALU.add
                                        ).then_inc(pchain, 1)
                pool.wait_ge(pchain, lay * POOL_LINKS + (link + 1))
                power(lay, link + 1, (rstd[:, which, :], sx[:, which, :], neg_half[:, 0, 0:MT]),
                      sx[:, which, :], 1.0 / D, EPS, x_norm)

            def load_bias(lay, g):
                if g >= 2:
                    for m in range(MT):
                        wait_emptied(pool, lay, (f"z{GATE_CHUNK + g - 2}", m))
                pool.dma_start(bias_sb[:, g % 2, :],
                               gate_v[lay * 6 + g:lay * 6 + g + 1, :].to_broadcast([P, NC])
                               ).then_inc(bias_loaded[g % 2], 16)

            for lay in range(DEPTH):
                pool.wait_ge(scaled, lay * len(SCALED_TURNS) + len(SCALED_TURNS))
                pool.dma_start(par[:, :], params_v[lay * P:lay * P + P, :]).then_inc(params_loaded, 16)
                load_bias(lay, 0)
                load_bias(lay, 1)
                x_norms(lay, 0, 0)
                n = 0
                for name, _, hs, first, _, _, _ in REGIONS:
                    mul, eps = (1.0, HD * EPS) if name[-1] == "q" else (1.0 / HD, EPS)
                    for m in range(MT):
                        pool.wait_ge(head_sums, lay * 8 + (n + 1))
                        h = slice(first, first + hs)
                        power(lay, 2 + n, (rs[:, m, h], rs_in[:, m, h], neg_half[:, m, h]),
                              ss[:, m, h], mul, eps, head_norms)
                        n += 1
                for g in range(2, 6):
                    load_bias(lay, g)
                x_norms(lay, 1, 10)

        @block.scalar
        def _(act):
            for b in range(0, 8):
                act.sem_inc(bank_free[b], 1)

            def split(lay, j):
                act.wait_ge(unit_landed[j % RING], lay * (16 * UNITS // RING) + 16 * (j // RING + 1))
                nc.scalar.activation(w_hi[:, j % RING, :, :].rearrange("p k n -> p (k n)"),
                                     w_raw[:, j % RING, :, :].rearrange("p k n -> p (k n)"),
                                     ACT.Copy).then_inc(unit_hi, 1)

            def turn(lay, name):
                kind, i = name
                if kind in SCALED:
                    n = SCALED_TURNS.index(name)
                    act.wait_ge(scaled, (lay + 1) * len(SCALED_TURNS) + (n + 1))
                    src = scratch[:, NC * (n % 2):NC * (n % 2) + NC]
                    nc.scalar.activation(turn_dest(name, True), turn_view(name, src), ACT.Copy
                                         ).then_inc(turn_hi, 1)
                    return
                wait_full(act, lay, name)
                if kind in SPLIT:
                    nc.scalar.activation(turn_dest(name, True), turn_view(name, B(name)[:, :]), ACT.Copy
                                         ).then_inc(turn_hi, 1)
                elif kind == "qk":
                    first, k = QK_BATCH[i]
                    free(nc.scalar.activation(qkT[:, first:first + k, :].rearrange("p k n -> p (k n)"),
                                              B(name)[:, 0:k * SEQ], ACT.Copy), name)
                elif kind == "probs":
                    free(nc.scalar.activation(probsT[:, i % 2, :], B(name)[:, :], ACT.Copy), name)
                else:
                    free(nc.scalar.activation(pooledT[:, 2 * i:2 * i + 2, :].rearrange("p k n -> p (k n)"),
                                              B(name)[:, :], ACT.Copy), name)

            def softmax_exp(lay, i):
                act.wait_ge(max_ready, lay * ATT + (i + 1))
                if i < 8:
                    m, h = i // 4, 2 * (i % 4)
                    nc.scalar.activation(probs[:, i % 2, 0:SEQ], B(("s", i))[:, 0:SEQ], ACT.Exp,
                                         bias=neg_max[:, 2 * i:2 * i + 1], accum_out=den[:, m, h:h + 1])
                    last = nc.scalar.activation(probs[:, i % 2, SEQ:NC], B(("s", i))[:, SEQ:NC], ACT.Exp,
                                                bias=neg_max[:, 2 * i + 1:2 * i + 2],
                                                accum_out=den[:, m, h + 1:h + 2])
                else:
                    m, s = (i - 8) // 4, i % 4
                    last = nc.scalar.activation(probs[:, i % 2, :], B(("s", i))[:, :], ACT.Exp,
                                                bias=neg_max[:, 2 * i:2 * i + 1],
                                                accum_out=den[:, m, 8 + s:9 + s])
                free(last, ("s", i))

            def x_squares(lay, m, half):
                room = (probs, probsT)[half][:, m, :]
                nc.scalar.activation(room, x_sb[:, m, NC * half:NC * half + NC], ACT.Square,
                                     accum_out=ssx[:, half, m:m + 1]).then_inc(x_sums, 1)

            act.wait_ge(const_loaded, 16)
            nc.scalar.activation(mask_sb[:, 0:P], ident, ACT.Copy).then_inc(mask_ready, 1)
            act.wait_ge(mask_loaded, 16)
            nc.scalar.activation(mask_sb[:, P:], gates[:, 0, 0:MT * NC], ACT.Copy).then_inc(mask_ready, 1)
            act.wait_ge(x_loaded, 16)
            with act.Fori(0, DEPTH) as lay:
                for t in range(UNITS):
                    if t == 0:
                        split(lay, 0)
                        for name in turn_batches(0):
                            turn(lay, name)
                        split(lay, 1)
                        for half in range(2):
                            for m in range(MT):
                                b = (2 if half == 0 else 0) + m
                                act.wait_ge(bank_free[b], lay * USES[b] + 1)
                                x_squares(lay, m, half)
                        continue
                    if 0 <= t - ATT_STEP < ATT:
                        softmax_exp(lay, t - ATT_STEP)
                    if t == 26:
                        for m in range(MT):
                            wait_emptied(act, lay, (f"z{Z_CHUNKS - 1}", m))
                        for n in range(2):
                            for m in range(MT):
                                nc.scalar.activation(gate_v3[:, m, :, n, :], gate_v3[:, m, :, n, :],
                                                     ACT.Sigmoid).then_inc(gate_done, 1)
                    for name in turn_batches(t):
                        turn(lay, name)
                    for j in splits_at(t):
                        split(lay, j)
                    if t % 2 == 1 and t // 2 <= POOL_CHUNK:
                        c = t // 2
                        if c == 0:
                            act.wait_ge(x_norm, lay * 2 + 1)
                        for m in range(MT):
                            wait_full(act, lay, (f"z{c}", m))
                            for off, w, to, at in Z_PIECES[c]:
                                dst = zqk if to == "qk" else zvu
                                last = nc.scalar.activation(dst[:, m, at:at + w],
                                                            B((f"z{c}", m))[:, off:off + w], ACT.Copy,
                                                            scale=rstd[:, 0, m:m + 1])
                            free(last, (f"z{c}", m))
                    if t == U_OUT + 3:
                        for half in range(2):
                            for m in range(MT):
                                wait_emptied(act, lay, (f"W{half}", m))
                                x_squares(lay, m, half)
                    i, odd = divmod(t - U_FFN, 2)
                    if 0 <= i < FC and odd:
                        if i == 0:
                            act.wait_ge(x_norm, lay * 2 + 2)
                        for m in range(MT):
                            wait_full(act, lay, (f"f{i}", m))
                            nc.scalar.activation(sg[:, i % 2, m, :], B((f"f{i}", m))[:, 0:256], ACT.Sigmoid,
                                                 scale=rstd[:, 1, m:m + 1]).then_inc(sig_done, 1)

        @block.vector
        def _(dve):
            links = [0]

            def link(ins):
                links[0] += 1
                ins.then_inc(vchain, 1)
                return links[0]

            def after(lay, n):
                dve.wait_ge(vchain, lay * VECTOR_LINKS + n)

            def split(lay, j):
                dve.wait_ge(unit_hi, lay * UNITS + (j + 1))
                w = [a[:, j % RING, :, :].rearrange("p k n -> p (k n)") for a in (w_lo, w_raw, w_hi)]
                nc.vector.tensor_tensor(w[0], w[1], w[2].bitcast(F32), ALU.subtract).then_inc(unit_lo, 1)

            def scale_turn(lay, name):
                kind, i = name
                n = SCALED_TURNS.index(name)
                wait_full(dve, lay, name)
                if kind == "mixed":
                    gain = par[:, PR_PS + 2 * i:PR_PS + 2 * i + 2].unsqueeze(2).to_broadcast([P, 2, SEQ])
                else:
                    first = (PR_MIX if kind == "mix_x" else PR_FFN) + UK * (i // 2)
                    gain = par[:, first:first + UK].unsqueeze(2).to_broadcast([P, UK, P])
                src = turn_view(name, B(name)[:, :])
                dst = turn_view(name, scratch[:, NC * (n % 2):NC * (n % 2) + NC])
                nc.vector.tensor_tensor(dst, src, gain, ALU.mult).then_inc(scaled, 1)

            def low_turn(lay, name):
                n = HI_TURNS.index(name)
                dve.wait_ge(turn_hi, lay * len(HI_TURNS) + (n + 1))
                hi = turn_dest(name, True).bitcast(F32)
                if name[0] in SCALED:
                    k = SCALED_TURNS.index(name)
                    src = scratch[:, NC * (k % 2):NC * (k % 2) + NC]
                    ins = nc.vector.tensor_tensor(turn_dest(name, False), turn_view(name, src), hi, ALU.subtract)
                    free(ins, name)
                else:
                    ins = nc.vector.tensor_tensor(turn_dest(name, False), turn_view(name, B(name)[:, :]), hi,
                                                  ALU.subtract)
                    free(ins, name)

            def turns(lay, t):
                names = [n for n in turn_batches(t) if n[0] in SCALED + SPLIT]
                for name in names:
                    if name[0] in SCALED:
                        scale_turn(lay, name)
                for name in names:
                    low_turn(lay, name)

            def rope_tables(lay):
                dve.wait_ge(params_loaded, (lay + 1) * 16)
                for k in range(4):
                    axial = k < 2
                    cos, sin = rope_const[:, 0 if axial else 2, :, :], rope_const[:, 1 if axial else 3, :, :]
                    g = par[:, PR_GAIN + HD * k:PR_GAIN + HD * (k + 1)]
                    link(nc.vector.tensor_tensor(rope[:, k, 0, :, :], cos,
                                                 g.unsqueeze(1).to_broadcast([P, MT, HD]), ALU.mult))
                    r = 2 if axial else 1
                    w = HD // (2 * r)
                    for half in range(2):
                        o = rope[:, k, 1, :, :].rearrange("p m (r h w) -> p m r h w", r=r, h=2)[:, :, :, half, :]
                        s = sin.rearrange("p m (r h w) -> p m r h w", r=r, h=2)[:, :, :, half, :]
                        gp = g.rearrange("p (r h w) -> p r h w", r=r, h=2)[:, :, 1 - half, :]
                        link(nc.vector.tensor_tensor(o, s, gp.unsqueeze(1).to_broadcast([P, MT, r, w]), ALU.mult))
                return links[0]

            def rotate(lay, n, region, m, tables):
                name, col, hs, first, k, chunk, _ = region
                W = hs * HD
                z = zqk[:, m, col:col + W]
                t1, t2 = scratch[:, 0:W], scratch[:, B_W:B_W + W]
                wait_emptied(dve, lay, (f"z{chunk}", m))
                if n:
                    dve.wait_ge(rotated, lay * 8 + n)
                sq = link(nc.vector.tensor_tensor(t1, z, z, ALU.mult))
                r = 2 if k < 2 else 1
                w = HD // (2 * r)
                after(lay, tables)
                for half in range(2):
                    def part(a, h):
                        return a.rearrange("p (q r h w) -> p q r h w", r=r, h=2, w=w)[:, :, :, h, :]
                    table = rope[:, k, 1, m, :].rearrange("p (r h w) -> p r h w", r=r, h=2)[:, :, half, :]
                    turned = nc.vector.tensor_tensor(part(t2, half), part(z, 1 - half),
                                                     table.unsqueeze(1).to_broadcast([P, hs, r, w]), ALU.mult)
                turned = link(turned)
                after(lay, sq)
                nc.vector.tensor_reduce(ss[:, m, first:first + hs], t1.rearrange("p (h d) -> p h d", d=HD), AX_X,
                                        ALU.add).then_inc(head_sums, 1)
                dve.wait_ge(head_sums, lay * 8 + (n + 1))
                c = link(nc.vector.tensor_tensor(t1.rearrange("p (h d) -> p h d", d=HD),
                                                 z.rearrange("p (h d) -> p h d", d=HD),
                                                 rope[:, k, 0, m, :].unsqueeze(1).to_broadcast([P, hs, HD]),
                                                 ALU.mult))
                after(lay, c)
                s = link(nc.vector.tensor_tensor(t1, t1, t2, ALU.add))
                after(lay, s)
                dve.wait_ge(head_norms, lay * 8 + (n + 1))
                if name == "a_q":
                    dst = z.rearrange("p (j g d) -> p g j d", g=2, d=HD)
                    src = t1.rearrange("p (g j d) -> p g j d", g=2, d=HD)
                    nrm = rs[:, m, first:first + hs].rearrange("p (g j) -> p g j", g=2)
                    for g in range(2):
                        last = nc.vector.tensor_tensor(
                            dst[:, g, :, :], src[:, g, :, :],
                            nrm[:, g, :].unsqueeze(2).to_broadcast([P, 4, HD]), ALU.mult)
                else:
                    last = nc.vector.tensor_tensor(
                        z.rearrange("p (h d) -> p h d", d=HD), t1.rearrange("p (h d) -> p h d", d=HD),
                        rs[:, m, first:first + hs].unsqueeze(2).to_broadcast([P, hs, HD]), ALU.mult)
                last.then_inc(rotated, 1)

            def row_max(lay, i):
                wait_full(dve, lay, ("s", i))
                k = 2 if i < 8 else 1
                nc.vector.tensor_reduce(neg_max[:, 2 * i:2 * i + k],
                                        B(("s", i))[:, :].rearrange("p (h n) -> p h n", h=k), AX_X, ALU.max,
                                        negate=True).then_inc(max_ready, 1)

            def norm_heads(lay, o):
                m, h0, hs = o % 2, (0 if o < 2 else 8), (8 if o < 2 else SLOTS)
                wait_full(dve, lay, ("o", o))
                r = link(nc.vector.reciprocal(rden[:, m, h0:h0 + hs], den[:, m, h0:h0 + hs]))
                after(lay, r)
                free(nc.vector.tensor_tensor(
                    heads[:, m, h0 * HD:(h0 + hs) * HD].rearrange("p (h d) -> p h d", d=HD),
                    B(("o", o))[:, 0:hs * HD].rearrange("p (h d) -> p h d", d=HD),
                    rden[:, m, h0:h0 + hs].unsqueeze(2).to_broadcast([P, hs, HD]), ALU.mult), ("o", o))

            def merge(lay, branch, n, written):
                for m in range(MT):
                    name = ("ABC"[branch] + str(n), m)
                    wait_full(dve, lay, name)
                    if branch == 2:
                        dve.wait_ge(gate_done, lay * 4 + (2 * n + m + 1))
                    gate = gates[:, m, D * branch + NC * n:D * branch + NC * n + NC]
                    to = merged[:, m, NC * n:NC * n + NC]
                    if branch == 2:
                        free(nc.vector.tensor_tensor(to, B(name)[:, :], gate, ALU.mult), name)
                    else:
                        if (branch, n) in ((1, 0), (0, 1)):
                            after(lay, written[(branch, n) == (0, 1)][m])
                        elif (branch, n) == (1, 1):
                            dve.wait_ge(merged_ready, lay * 4 + (m + 1))
                        tmp = scratch[:, NC * m:NC * m + NC]
                        free(nc.vector.tensor_tensor(tmp, B(name)[:, :], gate, ALU.mult), name)
                for m in range(MT):
                    if branch == 2:
                        continue
                    name = ("ABC"[branch] + str(n), m)
                    wait_emptied(dve, lay, name)
                    if written[n][m] is None:
                        wait_emptied(dve, lay, (f"C{n}", m))
                    else:
                        after(lay, written[n][m])
                    to = merged[:, m, NC * n:NC * n + NC]
                    ins = nc.vector.tensor_tensor(to, to, scratch[:, NC * m:NC * m + NC], ALU.add)
                    if written[n][m] is None:
                        written[n][m] = link(ins)
                    else:
                        ins.then_inc(merged_ready, 1)

            def add_x(lay, name, n):
                for m in range(MT):
                    wait_full(dve, lay, (name, m))
                    part = x_sb[:, m, NC * n:NC * n + NC]
                    free(nc.vector.tensor_tensor(part, B((name, m))[:, :], part, ALU.add), (name, m))

            dve.wait_ge(x_loaded, 16)
            dve.wait_ge(const_loaded, 16)
            dve.sem_inc(scaled, len(SCALED_TURNS))
            with dve.Fori(0, DEPTH) as lay:
                links[0] = 0
                written = [[None] * MT, [None] * MT]
                for t in range(UNITS):
                    if t == 0:
                        split(lay, 0)
                        dve.wait_ge(params_loaded, (lay + 1) * 16)
                    if 0 <= t - ATT_STEP < ATT:
                        row_max(lay, t - ATT_STEP)
                    if t in (15, 19, 23, 27):
                        norm_heads(lay, (t - 15) // 4)
                    turns(lay, t)
                    for j in splits_at(t):
                        split(lay, j)
                    if t == 1:
                        tables = rope_tables(lay)
                    for r, region in enumerate(REGIONS):
                        for m in range(MT):
                            if region[-1][m] == t:
                                rotate(lay, 2 * r + m, region, m, tables)
                    c, odd = divmod(t, 2)
                    if odd and GATE_CHUNK <= c < Z_CHUNKS:
                        g = c - GATE_CHUNK
                        dve.wait_ge(bias_loaded[g % 2], lay * 48 + 16 * (g // 2 + 1))
                        for m in range(MT):
                            wait_full(dve, lay, (f"z{c}", m))
                            free(nc.vector.scalar_tensor_tensor(
                                gates[:, m, NC * g:NC * g + NC], B((f"z{c}", m))[:, :], rstd[:, 0, m:m + 1],
                                bias_sb[:, g % 2, :], ALU.mult, ALU.add), (f"z{c}", m))
                    for unit, branch, n in ((U_C0, 2, 0), (U_C1, 2, 1), (U_A0, 0, 0), (U_B, 1, 0), (U_B, 1, 1),
                                            (U_A1, 0, 1)):
                        if t == unit:
                            merge(lay, branch, n, written)
                    if t == U_OUT + 3:
                        add_x(lay, "W0", 0)
                        add_x(lay, "W1", 1)
                    i, odd = divmod(t - U_FFN, 2)
                    if 0 <= i < FC and odd:
                        made = []
                        for m in range(MT):
                            dve.wait_ge(sig_done, lay * 2 * FC + (2 * i + m + 1))
                            made.append(link(nc.vector.scalar_tensor_tensor(
                                scratch[:, 2 * NC + 256 * m:2 * NC + 256 * m + 256], B((f"f{i}", m))[:, 0:256],
                                rstd[:, 1, m:m + 1], sg[:, i % 2, m, :], ALU.mult, ALU.mult)))
                        for m in range(MT):
                            after(lay, made[m])
                            free(nc.vector.scalar_tensor_tensor(
                                hid[:, i % 2, m, :], B((f"f{i}", m))[:, 256:NC], rstd[:, 1, m:m + 1],
                                scratch[:, 2 * NC + 256 * m:2 * NC + 256 * m + 256], ALU.mult, ALU.mult),
                                (f"f{i}", m))
                    if t == U_DOWN + 5:
                        add_x(lay, "D0", 0)
                    if t == U_DOWN + 10:
                        add_x(lay, "D1", 1)
                assert links[0] == VECTOR_LINKS, links[0]

        @block.tensor
        def _(pe):
            pe.sem_inc(unit_done, RING)

            def product(out_ap, hi, lo, slot, k, start, stop, cols=slice(0, NC)):
                nc.tensor.matmul(out_ap, hi, w_lo[:, slot, k, cols], start=start, stop=False)
                nc.tensor.matmul(out_ap, hi, w_hi[:, slot, k, cols], start=False, stop=False)
                return nc.tensor.matmul(out_ap, lo, w_hi[:, slot, k, cols], start=False, stop=stop)

            def unit(lay, t):
                pe.wait_ge(unit_lo, lay * UNITS + (t + 1))

            def rows(t, name, m, hi, lo, tiles, wk, first, final):
                tok = slice(P * m, P * m + P)
                for i, k in enumerate(tiles):
                    last = product(B((name, m))[:, :], hi[:, k, tok], lo[:, k, tok], t % RING, wk + i,
                                   first and i == 0, final and i == len(tiles) - 1)
                if final:
                    full(last, (name, m))
                return last

            def half_unit(lay, t, name, src, tiles, first, final, wk=0):
                for m in range(MT):
                    if first:
                        wait_free(pe, lay, (name, m))
                    last = rows(t, name, m, src[0], src[1], tiles, wk, first, final)
                return last

            def transposes(lay, name):
                kind, i = name
                b = B(name)
                wait_free(pe, lay, name)

                def turn(at, src):
                    return nc.tensor.transpose(b[:, at:at + P], src, ident)

                if kind in ("mix_x", "ffn_x"):
                    half, m = divmod(i, 2)
                    if kind == "mix_x":
                        fb = (2 if half == 0 else 0) + m
                        pe.wait_ge(bank_free[fb], lay * USES[fb] + 1)
                    else:
                        wait_emptied(pe, lay, (f"W{half}", m))
                    for k in range(UK):
                        last = turn(P * k, x_sb[:, m, P * (UK * half + k):P * (UK * half + k + 1)])
                elif kind == "merged":
                    half, m = divmod(i, 2)
                    pe.wait_ge(merged_ready, lay * 4 + (i + 1))
                    for k in range(UK):
                        last = turn(P * k, merged[:, m, P * (UK * half + k):P * (UK * half + k + 1)])
                elif kind == "qk":
                    first, k = QK_BATCH[i]
                    region = 0 if i < 2 else 1 if i < 3 else 2 if i < 6 else 3
                    pe.wait_ge(rotated, lay * 8 + 2 * (region + 1))
                    for j in range(k):
                        for m in range(MT):
                            last = turn(P * (2 * j + m), zqk[:, m, P * (first + j):P * (first + j + 1)])
                elif kind == "probs":
                    wait_emptied(pe, lay, ("s", i))
                    for c in range(4):
                        last = turn(P * c, probs[:, i % 2, P * c:P * c + P])
                elif kind == "heads":
                    wait_emptied(pe, lay, ("o", i))
                    m, c0, k = i % 2, (0 if i < 2 else A_Q), (4 if i < 2 else 2)
                    for c in range(k):
                        last = turn(P * c, heads[:, m, c0 + P * c:c0 + P * c + P])
                elif kind == "hidden":
                    for m in range(MT):
                        wait_emptied(pe, lay, (f"f{i}", m))
                    for k in range(2):
                        for m in range(MT):
                            last = turn(P * (2 * k + m), hid[:, i % 2, m, P * k:P * k + P])
                elif kind == "pool":
                    if i == 0:
                        for m in range(MT):
                            wait_emptied(pe, lay, (f"z{POOL_CHUNK}", m))
                    for g in (2 * i, 2 * i + 1):
                        for m in range(MT):
                            last = nc.tensor.matmul(b[:, SEQ * (g % 2):SEQ * (g % 2) + SEQ],
                                                    zvu[:, m, VU_POOL + P * g:VU_POOL + P * g + P],
                                                    pool_mat[:, m, g, :], start=(m == 0), stop=(m == MT - 1))
                else:
                    wait_emptied(pe, lay, ("pool", i))
                    for g in (2 * i, 2 * i + 1):
                        last = nc.tensor.matmul(b[:, SEQ * (g % 2):SEQ * (g % 2) + SEQ], lin[:, g, :],
                                                pooledT[:, g, :], start=True, stop=True)
                full(last, name)

            def scores(lay, i):
                wait_free(pe, lay, ("s", i))
                b = B(("s", i))
                if i == 0:
                    wait_emptied(pe, lay, ("qk", 2))
                if i == 8:
                    wait_emptied(pe, lay, ("qk", 7))
                    wait_emptied(pe, lay, ("qk", 8))
                if i < 8:
                    m, (g, pair) = i // 4, divmod(i % 4, 2)
                    part = slice(HD * g, HD * g + HD)
                    for hh in range(2):
                        last = nc.tensor.matmul(b[:, SEQ * hh:SEQ * hh + SEQ],
                                                qkT[part, QT_A_Q + 2 * pair + hh, P * m:P * m + P],
                                                qkT[part, QT_A_K, :], start=True, stop=True)
                else:
                    m, s = (i - 8) // 4, i % 4
                    nc.tensor.matmul(b[:, :], ident_b, mask_m[m], start=True, stop=False)
                    part = slice(HD * (s % 2), HD * (s % 2) + HD)
                    for g in range(GROUPS):
                        tile = 2 * g + s // 2
                        cols, keys = (slice(0, SEQ), slice(0, SEQ)) if g == 0 else \
                            (slice(SEQ + P * (g - 1), SEQ + P * g), slice(P * m, P * m + P))
                        last = nc.tensor.matmul(b[:, cols], qkT[part, QT_B_Q + tile, P * m:P * m + P],
                                                qkT[part, QT_B_K + tile, keys], start=False,
                                                stop=(g == GROUPS - 1))
                full(last, ("s", i))

            def values(lay, i):
                wait_emptied(pe, lay, ("probs", i))
                if i < 8:
                    m, h, o = i // 4, 2 * (i % 4), i // 4
                    todo = [(h + hh, [(2 * hh + kt, kt, VU_A + HD * ((h + hh) // 4)) for kt in range(MT)])
                            for hh in range(2)]
                else:
                    m, s, o = (i - 8) // 4, i % 4, 2 + (i - 8) // 4
                    v = [VU_B + HD * (SLOTS * g + s) for g in range(GROUPS)]
                    todo = [(s, [(0, 0, v[0]), (1, 1, v[0]), (2, m, v[1]), (3, m, v[2])])]
                if i % 4 == 0:
                    wait_free(pe, lay, ("o", o))
                for h, terms in todo:
                    for n, (c, kt, col) in enumerate(terms):
                        last = nc.tensor.matmul(B(("o", o))[:, HD * h:HD * h + HD],
                                                probsT[:, i % 2, P * c:P * c + P], zvu[:, kt, col:col + HD],
                                                start=(n == 0), stop=(n == len(terms) - 1))
                if i % 4 == 3:
                    full(last, ("o", o))

            aT, oT, mixT, hT = (aT_hi, aT_lo), (oT_hi, oT_lo), (mixT_hi, mixT_lo), (hT_hi, hT_lo)
            pe.wait_ge(x_loaded, 16)
            pe.wait_ge(const_loaded, 16)
            pe.wait_ge(mask_ready, 2)
            with pe.Fori(0, DEPTH) as lay:
                for t in range(UNITS):
                    for name in turn_batches(t):
                        if name[0] == "probs":
                            transposes(lay, name)
                    if 0 <= t - ATT_STEP < ATT:
                        scores(lay, t - ATT_STEP)
                    if 0 <= t - ATT_STEP - 2 < ATT:
                        values(lay, t - ATT_STEP - 2)
                    for name in turn_batches(t):
                        if name[0] != "probs":
                            transposes(lay, name)
                    unit(lay, t)
                    if t < U_C0:
                        c, half = divmod(t, 2)
                        if c == 0:
                            for m in range(MT):
                                wait_emptied(pe, lay, ("mix_x", 2 * half + m))
                        last = half_unit(lay, t, f"z{c}", aT, range(UK * half, UK * half + UK), half == 0, half == 1)
                    elif t in (U_C0, U_C1):
                        if t == U_C0:
                            for i in range(2):
                                wait_emptied(pe, lay, ("mixed", i))
                        last = half_unit(lay, t, f"C{t - U_C0}", mixT, range(4), True, True)
                    elif t in (U_A0, U_A1):
                        if t == U_A0:
                            wait_emptied(pe, lay, ("heads", 0))
                            wait_emptied(pe, lay, ("heads", 1))
                        last = half_unit(lay, t, "A0" if t == U_A0 else "A1", oT, range(4), True, True)
                    elif t == U_B:
                        wait_emptied(pe, lay, ("heads", 2))
                        wait_emptied(pe, lay, ("heads", 3))
                        half_unit(lay, t, "B0", oT, (4, 5), True, True)
                        last = half_unit(lay, t, "B1", oT, (4, 5), True, True, wk=2)
                    elif t < U_FFN:
                        half, n = divmod(t - U_OUT, 2)
                        if n == 0:
                            for m in range(MT):
                                wait_emptied(pe, lay, ("merged", 2 * half + m))
                        last = half_unit(lay, t, f"W{n}", aT, range(UK * half, UK * half + UK), half == 0, half == 1)
                    elif t < U_DOWN:
                        i, half = divmod(t - U_FFN, 2)
                        if i == 0:
                            for m in range(MT):
                                wait_emptied(pe, lay, ("ffn_x", 2 * half + m))
                        last = half_unit(lay, t, f"f{i}", aT, range(UK * half, UK * half + UK), half == 0, half == 1)
                    else:
                        q = t - U_DOWN
                        if q < 5:
                            for i in (2 * q, 2 * q + 1):
                                wait_emptied(pe, lay, ("hidden", i))
                            last = half_unit(lay, t, "D0", hT, range(UK * q, UK * q + UK), q == 0, False)
                        elif q == 5:
                            wait_emptied(pe, lay, ("hidden", FC - 1))
                            half_unit(lay, t, "D0", hT, (20, 21), False, True)
                            last = half_unit(lay, t, "D1", hT, (20, 21), True, False, wk=2)
                        else:
                            q -= 6
                            last = half_unit(lay, t, "D1", hT, range(UK * q, UK * q + UK), False, q == 4)
                    last.then_inc(unit_done, 1)


def constants():
    import numpy as np
    tok = np.stack([2 * np.arange(P) + m for m in range(MT)])
    flat = tok.reshape(-1)

    def angles(pos, dim):
        inv = np.float32(10000.0) ** (-np.arange(0, dim, 2, dtype=np.float32) / np.float32(dim))
        return (pos.astype(np.float32)[..., None] * inv.astype(np.float32)).astype(np.float32)

    def table(parts):
        cos = np.concatenate([np.concatenate([np.cos(a), np.cos(a)], -1) for a in parts], -1)
        sin = np.concatenate([np.concatenate([-np.sin(a), np.sin(a)], -1) for a in parts], -1)
        return cos, sin

    axial = table([angles(tok // 64, HD // 2), angles(tok % 64, HD // 2)])
    plain = table([angles(tok, HD)])
    rope = np.stack([axial[0], axial[1], plain[0], plain[1]])
    pool = np.zeros((SEQ, POOL_G, SEQ), np.float32)
    for g, w in enumerate((2, 4, 8, 16)):
        for n, t in enumerate(flat):
            lo, hi = max(t - w // 2, 0), min(t + w - w // 2, SEQ)
            inside = (flat >= lo) & (flat < hi)
            pool[inside, g, n] = np.float32(1.0) / np.float32(hi - lo)
            pool[n, g, n] -= np.float32(1.0)
    con = np.concatenate([
        np.eye(P, dtype=np.float32),
        rope.transpose(2, 0, 1, 3).reshape(P, -1).astype(np.float32),
        pool.reshape(MT, P, POOL_G, SEQ).transpose(1, 0, 2, 3).reshape(P, -1)], 1)
    masks = []
    for m in range(MT):
        q = tok[m][:, None]
        masks.append(np.concatenate([
            np.where(np.abs(q - flat[None, :]) <= 64, 0.0, NEG_INF),
            np.where((q - tok[m][None, :]) % 4 == 0, 0.0, NEG_INF),
            np.where((q - tok[m][None, :]) % 16 == 0, 0.0, NEG_INF)], 1))
    return np.ascontiguousarray(con, np.float32), np.concatenate(masks, 1).astype(np.float32)


def weight_stream(w_in, w_branch_a, w_branch_b, w_branch_c, w_out, w_ffn_gate, w_ffn_up, w_ffn_down):
    import numpy as np
    units = np.empty((DEPTH, UNITS, P, UK, NC), np.float32)
    for l in range(DEPTH):
        u = units[l]
        w = w_in[l].reshape(2, UK, P, Z_CHUNKS, NC)
        u[:U_C0] = w.transpose(3, 0, 2, 1, 4).reshape(2 * Z_CHUNKS, P, UK, NC)
        c = w_branch_c[l].reshape(UK, P, 2, NC)
        a = w_branch_a[l].reshape(UK, P, 2, NC)
        for n, (uc, ua) in enumerate(((U_C0, U_A0), (U_C1, U_A1))):
            u[uc] = c[:, :, n].transpose(1, 0, 2)
            u[ua] = a[:, :, n].transpose(1, 0, 2)
        b = w_branch_b[l].reshape(2, P, 2, NC)
        u[U_B] = b.transpose(1, 2, 0, 3).reshape(P, UK, NC)
        w = w_out[l].reshape(2, UK, P, 2, NC)
        u[U_OUT:U_FFN] = w.transpose(0, 3, 2, 1, 4).reshape(4, P, UK, NC)
        for at, w in ((0, w_ffn_gate[l]), (256, w_ffn_up[l])):
            w = w.reshape(2, UK, P, FC, 256).transpose(3, 0, 2, 1, 4)
            u[U_FFN:U_DOWN, :, :, at:at + 256] = w.reshape(2 * FC, P, UK, 256)
        w = w_ffn_down[l].reshape(KF, P, 2, NC)
        for n, first in ((0, U_DOWN), (1, U_DOWN + 6)):
            u[first:first + 5] = w[:20, :, n].reshape(5, UK, P, NC).transpose(0, 2, 1, 3)
        u[U_DOWN + 5] = w[20:].transpose(1, 2, 0, 3).reshape(P, UK, NC)
    return units.reshape(DEPTH * UNITS, P, UNIT)


def layer_params(norm_mix, norm_ffn, pool_scale, qn_a, kn_a, qn_b, kn_b, pool_lin):
    import numpy as np
    par = np.empty((DEPTH, P, PR_W), np.float32)
    par[:, :, PR_MIX:PR_MIX + KT] = norm_mix.reshape(DEPTH, KT, P).transpose(0, 2, 1)
    par[:, :, PR_FFN:PR_FFN + KT] = norm_ffn.reshape(DEPTH, KT, P).transpose(0, 2, 1)
    par[:, :, PR_PS:PR_PS + POOL_G] = pool_scale.reshape(DEPTH, POOL_G, P).transpose(0, 2, 1)
    for k, g in enumerate((qn_a, kn_a, qn_b, kn_b)):
        par[:, :, PR_GAIN + HD * k:PR_GAIN + HD * (k + 1)] = g[:, None, :]
    par[:, :, PR_LIN:] = pool_lin.transpose(0, 2, 1, 3).reshape(DEPTH, P, POOL_G * P)
    return par


def kernel(**inputs):
    import numpy as np
    import concourse.bacc as bacc
    from concourse.bass_utils import run_bass_kernel_spmd

    i = {k: np.asarray(v) for k, v in inputs.items()}
    con, mask = constants()
    host = {
        "x": np.ascontiguousarray(i["x"]),
        "stream": weight_stream(i["w_in"], i["w_branch_a"], i["w_branch_b"], i["w_branch_c"], i["w_out"],
                                i["w_ffn_gate"], i["w_ffn_up"], i["w_ffn_down"]),
        "params": layer_params(i["norm_mix"], i["norm_ffn"], i["pool_scale"], i["qn_a"], i["kn_a"], i["qn_b"],
                               i["kn_b"], i["pool_lin"]),
        "b_gate": np.ascontiguousarray(i["b_gate"].reshape(DEPTH, 3 * D // NC, NC)),
        "const": con,
        "mask": mask,
    }
    nc = bacc.Bacc("TRN2", target_bir_lowering=False, num_devices=1, dynamic_dma_scratch_size=4096)
    arrays, args = {}, []
    for name, a in host.items():
        arrays[f"in_{name}_dram"] = a
        args.append(nc.dram_tensor(f"in_{name}_dram", a.shape, mybir.dt.from_np(a.dtype), kind="ExternalInput").ap())
    args.append(nc.dram_tensor("out_0_dram", (1, SEQ, D), F32, kind="ExternalOutput").ap())
    build(nc, *args)
    r = run_bass_kernel_spmd(nc, [arrays], core_ids=[0])
    return r.results[0]["out_0_dram"]
```

```python
from contextlib import ExitStack

import concourse.bass as bass
from concourse import mybir

F32 = mybir.dt.float32
F32R = mybir.dt.float32r
BF16 = mybir.dt.bfloat16
ALU = mybir.AluOpType
ACT = mybir.ActivationFunctionType
AX_X = mybir.AxisListType.X

P = 128
DEPTH, SEQ, D = 2, 256, 1024
HD = 64
EPS = 1e-6
NEG_INF = -1e30
MT = SEQ // P
KT = D // P
NC = 512
UK = 4
UNIT = UK * NC
D_FF = 2816
A_Q, A_KV, B_W, POOL_W = 512, 128, 768, 512
GROUPS, SLOTS = 3, 4
POOL_G = 4
Z_CHUNKS, GATE_CHUNK, POOL_CHUNK = 13, 7, 6
FC = D_FF // 256
KF = D_FF // P
RING = 4

U_Z = 0
U_C0, U_C1, U_A0, U_B, U_A1 = 26, 27, 28, 29, 30
U_OUT = 31
U_FFN = 35
U_DOWN = U_FFN + 2 * FC
UNITS = U_DOWN + 11
assert UNITS % RING == 0

QK_A_Q, QK_A_K, QK_B_Q, QK_B_K = 0, 512, 640, 1408
QK_W = 2176
VU_A, VU_B, VU_POOL = 0, 128, 896
VU_W = 1408
Z_PIECES = [
    [(0, 512, "qk", 0)],
    [(0, 128, "qk", 512), (128, 128, "vu", 0), (256, 256, "qk", 640)],
    [(0, 512, "qk", 896)],
    [(0, 512, "qk", 1408)],
    [(0, 256, "qk", 1920), (256, 256, "vu", 128)],
    [(0, 512, "vu", 384)],
    [(0, 512, "vu", 896)],
]
REGIONS = [
    ("a_q", QK_A_Q, 8, 0, 0, 0, (2, 3)),
    ("a_k", QK_A_K, 2, 8, 1, 1, (4, 4)),
    ("b_q", QK_B_Q, 12, 10, 2, 2, (6, 7)),
    ("b_k", QK_B_K, 12, 22, 3, 4, (10, 11)),
]
HEADS = 34
QT_A_Q, QT_A_K, QT_B_Q, QT_B_K, QTILES = 0, 4, 5, 11, 17

PR_MIX, PR_FFN, PR_PS, PR_GAIN, PR_LIN = 0, 8, 16, 20, 20 + 4 * HD
PR_W = PR_LIN + POOL_G * P

ATT = 16
ATT_STEP = 9

TURNS_BEFORE = {
    6: [("qk", 0)], 7: [("qk", 2)], 14: [("qk", 7)], 28: [("heads", 3)],
    32: [("merged", 2), ("merged", 3)],
    U_DOWN + 7: [("mix_x", 0), ("mix_x", 1)],
}
TURNS_WITHIN = {
    0: [("mix_x", 2), ("mix_x", 3)], 6: [("qk", 1)],
    10: [("qk", 3)], 11: [("qk", 4)], 12: [("qk", 5)], 13: [("qk", 6)], 14: [("qk", 8)],
    16: [("heads", 0)], 17: [("pool", 0)], 18: [("pool", 1)], 20: [("mixed", 0)], 21: [("mixed", 1)],
    22: [("heads", 1)], 25: [("heads", 2)], 30: [("merged", 0), ("merged", 1)],
    U_OUT + 3: [("ffn_x", 0), ("ffn_x", 1)], U_FFN: [("ffn_x", 2), ("ffn_x", 3)],
}


def turns_before(t):
    out = []
    if 0 <= t - ATT_STEP - 2 < ATT:
        out.append(("probs", t - ATT_STEP - 2))
    out += TURNS_BEFORE.get(t, [])
    i, odd = divmod(t - U_FFN - 3, 2)
    if 0 <= i < FC and not odd:
        out.append(("hidden", i))
    return out


def turns_within(t):
    return TURNS_WITHIN.get(t, [])


QK_BATCH = [(0, 2), (2, 2), (4, 1), (5, 2), (7, 2), (9, 2), (11, 2), (13, 2), (15, 2)]
SCALED = ("mix_x", "mixed", "ffn_x")
SPLIT = ("heads", "merged", "hidden")
PLAIN = ("qk", "probs", "pool")


def plan_banks():
    order = {b: [] for b in range(8)}

    def pair(first, name):
        for m in range(MT):
            order[first + m].append((name, m))

    for c in range(Z_CHUNKS):
        pair(2 if c in (0, 2, 4) else 0, f"z{c}")
    order[2] += [("o", 0), ("o", 2)]
    order[3] += [("o", 1), ("o", 3)]
    for i in range(ATT):
        order[4 + i % 2].append(("s", i))
    pair(4, "C1")
    pair(0, "C0")
    pair(0, "A0")
    pair(2, "B0")
    pair(4, "B1")
    pair(0, "A1")
    pair(2, "W0")
    pair(4, "W1")
    for i in range(FC):
        pair(2 * (i % 2), f"f{i}")
    pair(2, "D0")
    pair(0, "D1")
    n = 0
    for t in range(UNITS):
        for b in turns_before(t) + turns_within(t):
            order[6 + n % 2].append(b)
            n += 1
    assert n % 2 == 0
    use = {name: (b, k) for b, names in order.items() for k, name in enumerate(names)}
    return order, use, {b: len(names) for b, names in order.items()}


ORDER, USE, USES = plan_banks()

UNIT_ENDS = {(f"z{c}", 1): 2 * c + 1 for c in range(Z_CHUNKS)}
UNIT_ENDS |= {("C0", 1): U_C0, ("C1", 1): U_C1, ("A0", 1): U_A0, ("B1", 1): U_B, ("A1", 1): U_A1,
              ("W0", 1): U_OUT + 2, ("W1", 1): U_OUT + 3, ("D1", 1): U_DOWN + 10}
UNIT_ENDS |= {(f"f{i}", 1): U_FFN + 2 * i + 1 for i in range(FC)}
FULL = {name: n for b in ORDER for n, name in enumerate([x for x in ORDER[b] if x not in UNIT_ENDS])}
FULLS = {b: len([x for x in names if x not in UNIT_ENDS]) for b, names in ORDER.items()}

HI_TURNS = [b for t in range(UNITS) for b in turns_before(t) + turns_within(t) if b[0] in SCALED + SPLIT]
SCALED_TURNS = [b for b in HI_TURNS if b[0] in SCALED]
EARLY = {b: int(b >= 6) for b in range(8)}
EARLY_TURNS = 2
BEFORE = -1
VECTOR_LINKS = 12 + 8 * 4 + 4 + 2 * MT + MT * FC
POOL_LINKS = 12


def splits_at(t):
    if t == 0:
        return [1]
    if t == 1:
        return [2, 3]
    return [t + 2] if t + 2 < UNITS else []


def build(nc, x, stream, params, b_gate, eye, angles, pooling, mask, out):
    stream_v = stream.rearrange("u p n -> (u p) n")
    params_v = params.rearrange("l p n -> (l p) n")
    gate_v = b_gate.rearrange("l g n -> (l g) n")
    with ExitStack() as ctx:
        def sb(name, shape, dt=F32, to=ctx):
            return to.enter_context(nc.sbuf_tensor(name, shape, dt))

        def sem(name):
            return ctx.enter_context(nc.semaphore(name))

        w_hi = sb("w_hi", [P, RING, UK, NC], F32R)
        with ExitStack() as shared:
            w_raw = sb("w_raw", [P, RING, UK, NC], F32, shared)
        w_lo = sb("w_lo", [P, RING, UK, NC], F32R)
        x_sb = sb("x_sb", [P, MT, D])
        aT_hi = sb("aT_hi", [P, KT, SEQ], F32R)
        aT_lo = sb("aT_lo", [P, KT, SEQ], F32R)
        qkT = sb("qkT", [P, QTILES, SEQ])
        probs = sb("probs", [P, 2, NC])
        probsT = sb("probsT", [P, 2, NC])
        scratch = sb("scratch", [P, 2 * B_W])
        bias_sb = sb("bias_sb", [P, 2, NC])
        ident = sb("ident", [P, P])
        rope_c = sb("rope_c", [P, 4, MT, HD])
        pool_mat = sb("pool_mat", [P, MT, POOL_G, SEQ])
        mask_sb = sb("mask_sb", [P, P + MT * NC], BF16)
        rope = sb("rope", [P, 4, 2, MT, HD])
        par = sb("par", [P, PR_W])
        mixT_hi = sb("mixT_hi", [P, POOL_G, SEQ], F32R)
        mixT_lo = sb("mixT_lo", [P, POOL_G, SEQ], F32R)
        oT_hi = sb("oT_hi", [P, 6, SEQ], F32R)
        oT_lo = sb("oT_lo", [P, 6, SEQ], F32R)
        ss = sb("ss", [P, MT, HEADS])
        rs = sb("rs", [P, MT, HEADS])
        rs_in = sb("rs_in", [P, MT, HEADS])
        neg_half = sb("neg_half", [P, MT, HEADS])
        ssx = sb("ssx", [P, 2, MT])
        sx = sb("sx", [P, 2, MT])
        rstd = sb("rstd", [P, 2, MT])
        neg_max = sb("neg_max", [P, 2 * ATT])
        den = sb("den", [P, MT, 8 + SLOTS])
        rden = sb("rden", [P, MT, 8 + SLOTS])
        with ExitStack() as mixer:
            with ExitStack() as early:
                zqk = sb("zqk", [P, MT, QK_W], F32, early)
            with ExitStack() as late:
                heads = sb("heads", [P, MT, A_Q + SLOTS * HD], F32, late)
                merged = sb("merged", [P, MT, D], F32, late)
                pooledT = sb("pooledT", [P, POOL_G, SEQ], F32, late)
            sb("late_room", [P, MT * (A_Q + SLOTS * HD) + MT * D + POOL_G * SEQ], F32, mixer)
            zvu = sb("zvu", [P, MT, VU_W], F32, mixer)
            gates = sb("gates", [P, MT, 3 * D], F32, mixer)
        hT_hi = sb("hT_hi", [P, KF, SEQ], F32R)
        hT_lo = sb("hT_lo", [P, KF, SEQ], F32R)
        sg = sb("sg", [P, 2, MT, 256])
        hid = sb("hid", [P, 2, MT, 256])

        ident_b = mask_sb[:, 0:P]
        mask_m = [mask_sb[:, P + m * NC:P + (m + 1) * NC] for m in range(MT)]
        lin = par[:, PR_LIN:PR_W].rearrange("p (g d) -> p g d", g=POOL_G)
        gate_v3 = gates[:, :, :].rearrange("p m (b n c) -> p m b n c", b=3, n=2)

        bank = [ctx.enter_context(nc.psum_tensor(f"bank{b}", [P, NC], F32)) for b in range(8)]

        x0_loaded = sem("x0_loaded")
        x1_loaded = sem("x1_loaded")
        eye_loaded = sem("eye_loaded")
        angles_loaded = sem("angles_loaded")
        pooling_loaded = sem("pooling_loaded")
        mask_loaded = sem("mask_loaded")
        mask_ready = sem("mask_ready")
        params_loaded = sem("params_loaded")
        bias_loaded = [sem(f"bias_loaded{i}") for i in range(2)]
        unit_landed = [sem(f"unit_landed{i}") for i in range(RING)]
        unit_done = sem("unit_done")
        unit_hi = sem("unit_hi")
        unit_lo = sem("unit_lo")
        first_hi = sem("first_hi")
        first_lo = sem("first_lo")
        bank_full = [sem(f"bank_full{b}") for b in range(8)]
        bank_free = [sem(f"bank_free{b}") for b in range(8)]
        turn_hi = sem("turn_hi")
        turn_lo = sem("turn_lo")
        half_ready = sem("half_ready")
        head_sums = sem("head_sums")
        head_norms = sem("head_norms")
        rotated = sem("rotated")
        x_sums = sem("x_sums")
        x_norm = sem("x_norm")
        max_ready = sem("max_ready")
        exp_done = sem("exp_done")
        gate_done = sem("gate_done")
        merged_ready = sem("merged_ready")
        sig_done = sem("sig_done")
        vchain = sem("vchain")
        pchain = sem("pchain")
        out_done = sem("out_done")

        def B(name):
            return bank[USE[name][0]]

        def wait_free(eng, lay, name):
            b, k = USE[name]
            eng.wait_ge(bank_free[b], lay * USES[b] + (k + 1 + EARLY[b]))

        def wait_full(eng, lay, name):
            if name in UNIT_ENDS:
                eng.wait_ge(unit_done, lay * UNITS + (RING + UNIT_ENDS[name] + 1))
            else:
                b = USE[name][0]
                eng.wait_ge(bank_full[b], lay * FULLS[b] + (FULL[name] + 1 + EARLY[b]))

        def wait_emptied(eng, lay, name):
            b, k = USE[name]
            eng.wait_ge(bank_free[b], lay * USES[b] + (k + 2 + EARLY[b]))

        def full(ins, name):
            if name not in UNIT_ENDS:
                ins.then_inc(bank_full[USE[name][0]], 1)

        def free(ins, name):
            ins.then_inc(bank_free[USE[name][0]], 1)

        def wait_lo(eng, lay, name, former=False):
            n = SCALED_TURNS.index(name) + 1 + EARLY_TURNS - (len(SCALED_TURNS) if former else 0)
            eng.wait_ge(turn_lo, lay * len(SCALED_TURNS) + n)

        def turn_dest(name, hi):
            kind, i = name
            if kind in ("mix_x", "merged", "ffn_x"):
                to = aT_hi if hi else aT_lo
                return to[:, UK * (i // 2):UK * (i // 2) + UK, P * (i % 2):P * (i % 2) + P]
            if kind == "mixed":
                return (mixT_hi if hi else mixT_lo)[:, 2 * i:2 * i + 2, :]
            if kind == "heads":
                to, m = (oT_hi if hi else oT_lo), i % 2
                return to[:, 0:4, m * P:m * P + P] if i < 2 else to[:, 4:6, m * P:m * P + P]
            to = hT_hi if hi else hT_lo
            return to[:, 2 * i:2 * i + 2, :]

        def turn_view(name, ap):
            kind, i = name
            if kind in ("mix_x", "merged", "ffn_x"):
                return ap.rearrange("p (k n) -> p k n", k=UK)
            if kind == "heads":
                return ap.rearrange("p (k n) -> p k n", k=4) if i < 2 else \
                    ap[:, 0:2 * P].rearrange("p (k n) -> p k n", k=2)
            return ap.rearrange("p (k n) -> p k n", k=2)

        block = ctx.enter_context(nc.Block())

        @block.sync
        def _(sp):
            xv = x.rearrange("b (p m) d -> (b p) m d", m=MT)
            sp.dma_start(x_sb[:, :, 0:NC], xv[:, :, 0:NC]).then_inc(x0_loaded, 16)
            sp.dma_start(ident[:, :], eye).then_inc(eye_loaded, 16)
            sp.dma_start(x_sb[:, :, NC:D], xv[:, :, NC:D]).then_inc(x1_loaded, 16)
            with sp.Fori(0, DEPTH * UNITS // RING) as turn:
                for s in range(RING):
                    sp.wait_ge(unit_done, turn * RING + (s + 1))
                    sp.dma_start(w_raw[:, s, :, :].rearrange("p k n -> p (k n)"),
                                 stream_v[bass.ds((turn * RING + s) * P, P), :]
                                 ).then_inc(unit_landed[s], 16)
            for b in range(4):
                sp.wait_ge(bank_free[b], DEPTH * USES[b] + 1)
            ov = out.rearrange("b (p m) d -> (b p) m d", m=MT)
            sp.dma_start(ov, x_sb[:, :, :]).then_inc(out_done, 16)
            sp.wait_ge(out_done, 16)

        @block.gpsimd
        def _(pool):
            def load_params(layer):
                pool.dma_start(par[:, :], params_v[layer * P:layer * P + P, :]).then_inc(params_loaded, 16)

            load_params(0)
            pool.dma_start(rope_c[:, :, :, :].rearrange("p k m d -> p (k m d)"), angles
                           ).then_inc(angles_loaded, 16)
            pool.dma_start(gates[:, 0, 0:MT * NC], mask).then_inc(mask_loaded, 16)
            nc.gpsimd.memset(neg_half[:, :, :], -0.5).then_inc(half_ready, 1)
            pool.wait_ge(half_ready, 1)

            def power(lay, link, dst, src, mul, eps, signal):
                nc.gpsimd.tensor_scalar(dst[1], src, mul, eps, ALU.mult, ALU.add).then_inc(pchain, 1)
                pool.wait_ge(pchain, lay * POOL_LINKS + (link + 1))
                nc.gpsimd.tensor_tensor(dst[0], dst[1], dst[2], ALU.pow).then_inc(signal, 1)

            def x_norms(lay, which, link):
                pool.wait_ge(x_sums, lay * 8 + 4 * (which + 1))
                nc.gpsimd.tensor_tensor(sx[:, which, :], ssx[:, 0, :], ssx[:, 1, :], ALU.add
                                        ).then_inc(pchain, 1)
                pool.wait_ge(pchain, lay * POOL_LINKS + (link + 1))
                power(lay, link + 1, (rstd[:, which, :], sx[:, which, :], neg_half[:, 0, 0:MT]),
                      sx[:, which, :], 1.0 / D, EPS, x_norm)

            def load_bias(lay, g):
                if g >= 2:
                    for m in range(MT):
                        wait_emptied(pool, lay, (f"z{GATE_CHUNK + g - 2}", m))
                pool.dma_start(bias_sb[:, g % 2, :],
                               gate_v[lay * 6 + g:lay * 6 + g + 1, :].to_broadcast([P, NC])
                               ).then_inc(bias_loaded[g % 2], 16)

            for lay in range(DEPTH):
                load_bias(lay, 0)
                load_bias(lay, 1)
                x_norms(lay, 0, 0)
                if lay == 0:
                    pool.dma_start(pool_mat[:, :, :, :].rearrange("p m g n -> p (m g n)"), pooling
                                   ).then_inc(pooling_loaded, 16)
                n = 0
                for name, _, hs, first, _, _, _ in REGIONS:
                    mul, eps = (1.0, HD * EPS) if name[-1] == "q" else (1.0 / HD, EPS)
                    for m in range(MT):
                        pool.wait_ge(head_sums, lay * 8 + (n + 1))
                        h = slice(first, first + hs)
                        power(lay, 2 + n, (rs[:, m, h], rs_in[:, m, h], neg_half[:, m, h]),
                              ss[:, m, h], mul, eps, head_norms)
                        n += 1
                for g in range(2, 6):
                    load_bias(lay, g)
                x_norms(lay, 1, 10)
                wait_lo(pool, lay, ("ffn_x", 3))
                load_params(min(lay + 1, DEPTH - 1))

        @block.scalar
        def _(act):
            for b in range(0, 8):
                act.sem_inc(bank_free[b], 1)

            def split_first(lay):
                act.wait_ge(unit_landed[0], lay * (16 * UNITS // RING) + 16)
                for k in range(UK):
                    nc.scalar.activation(w_hi[:, 0, k, :], w_raw[:, 0, k, :], ACT.Copy).then_inc(first_hi, 1)

            def split(lay, j):
                act.wait_ge(unit_landed[j % RING], lay * (16 * UNITS // RING) + 16 * (j // RING + 1))
                nc.scalar.activation(w_hi[:, j % RING, :, :].rearrange("p k n -> p (k n)"),
                                     w_raw[:, j % RING, :, :].rearrange("p k n -> p (k n)"),
                                     ACT.Copy).then_inc(unit_hi, 1)

            def turn(lay, name):
                kind, i = name
                if kind in SCALED:
                    n = SCALED_TURNS.index(name)
                    wait_emptied(act, lay, name)
                    src = scratch[:, NC * (n % 2):NC * (n % 2) + NC]
                    nc.scalar.activation(turn_dest(name, True), turn_view(name, src), ACT.Copy
                                         ).then_inc(turn_hi, 1)
                    return
                wait_full(act, lay, name)
                if kind in SPLIT:
                    nc.scalar.activation(turn_dest(name, True), turn_view(name, B(name)[:, :]), ACT.Copy
                                         ).then_inc(turn_hi, 1)
                elif kind == "qk":
                    first, k = QK_BATCH[i]
                    free(nc.scalar.activation(qkT[:, first:first + k, :].rearrange("p k n -> p (k n)"),
                                              B(name)[:, 0:k * SEQ], ACT.Copy), name)
                elif kind == "probs":
                    free(nc.scalar.activation(probsT[:, i % 2, :], B(name)[:, :], ACT.Copy), name)
                else:
                    free(nc.scalar.activation(pooledT[:, 2 * i:2 * i + 2, :].rearrange("p k n -> p (k n)"),
                                              B(name)[:, :], ACT.Copy), name)

            def softmax_exp(lay, i):
                act.wait_ge(max_ready, lay * ATT + (i + 1))
                if i < 8:
                    m, h = i // 4, 2 * (i % 4)
                    nc.scalar.activation(probs[:, i % 2, 0:SEQ], B(("s", i))[:, 0:SEQ], ACT.Exp,
                                         bias=neg_max[:, 2 * i:2 * i + 1], accum_out=den[:, m, h:h + 1])
                    last = nc.scalar.activation(probs[:, i % 2, SEQ:NC], B(("s", i))[:, SEQ:NC], ACT.Exp,
                                                bias=neg_max[:, 2 * i + 1:2 * i + 2],
                                                accum_out=den[:, m, h + 1:h + 2])
                else:
                    m, s = (i - 8) // 4, i % 4
                    last = nc.scalar.activation(probs[:, i % 2, :], B(("s", i))[:, :], ACT.Exp,
                                                bias=neg_max[:, 2 * i:2 * i + 1],
                                                accum_out=den[:, m, 8 + s:9 + s])
                free(last, ("s", i))

            def x_squares(lay, m, half):
                room = (probs, probsT)[half][:, m, :]
                nc.scalar.activation(room, x_sb[:, m, NC * half:NC * half + NC], ACT.Square,
                                     accum_out=ssx[:, half, m:m + 1]).then_inc(x_sums, 1)

            act.wait_ge(x0_loaded, 16)
            for i in range(EARLY_TURNS):
                turn(BEFORE, ("mix_x", i))
            act.wait_ge(x1_loaded, 16)
            with act.Fori(0, DEPTH) as lay:
                for t in range(UNITS):
                    for name in turns_before(t):
                        turn(lay, name)
                    if 0 <= t - ATT_STEP < ATT:
                        softmax_exp(lay, t - ATT_STEP)
                    if t == 26:
                        for m in range(MT):
                            wait_emptied(act, lay, (f"z{Z_CHUNKS - 1}", m))
                        for n in range(2):
                            for m in range(MT):
                                nc.scalar.activation(gate_v3[:, m, :, n, :], gate_v3[:, m, :, n, :],
                                                     ACT.Sigmoid).then_inc(gate_done, 1)
                    if t == 0:
                        split_first(lay)
                    for j in splits_at(t):
                        split(lay, j)
                    for name in turns_within(t):
                        turn(lay, name)
                    if t == 0:
                        for half in range(2):
                            for m in range(MT):
                                b = (2 if half == 0 else 0) + m
                                act.wait_ge(bank_free[b], lay * USES[b] + 1)
                                x_squares(lay, m, half)
                    if t % 2 == 1 and t // 2 <= POOL_CHUNK:
                        c = t // 2
                        if c == 0:
                            act.wait_ge(x_norm, lay * 2 + 1)
                        for m in range(MT):
                            wait_full(act, lay, (f"z{c}", m))
                            for off, w, to, at in Z_PIECES[c]:
                                dst = zqk if to == "qk" else zvu
                                last = nc.scalar.activation(dst[:, m, at:at + w],
                                                            B((f"z{c}", m))[:, off:off + w], ACT.Copy,
                                                            scale=rstd[:, 0, m:m + 1])
                            free(last, (f"z{c}", m))
                    if t in (U_OUT + 3, U_FFN):
                        half = t - U_OUT - 3
                        for m in range(MT):
                            wait_emptied(act, lay, (f"W{half}", m))
                            x_squares(lay, m, half)
                    i, odd = divmod(t - U_FFN, 2)
                    if 0 <= i < FC and odd:
                        if i == 0:
                            act.wait_ge(x_norm, lay * 2 + 2)
                        for m in range(MT):
                            wait_full(act, lay, (f"f{i}", m))
                            nc.scalar.activation(sg[:, i % 2, m, :], B((f"f{i}", m))[:, 0:256], ACT.Sigmoid,
                                                 scale=rstd[:, 1, m:m + 1]).then_inc(sig_done, 1)

        @block.vector
        def _(dve):
            links = [0]

            def link(ins):
                links[0] += 1
                ins.then_inc(vchain, 1)
                return links[0]

            def after(lay, n):
                dve.wait_ge(vchain, lay * VECTOR_LINKS + n)

            def split(lay, j):
                dve.wait_ge(unit_hi, lay * (UNITS - 1) + j)
                w = [a[:, j % RING, :, :].rearrange("p k n -> p (k n)") for a in (w_lo, w_raw, w_hi)]
                nc.vector.tensor_tensor(w[0], w[1], w[2].bitcast(F32), ALU.subtract).then_inc(unit_lo, 1)

            def split_first(lay):
                for k in range(UK):
                    dve.wait_ge(first_hi, lay * UK + (k + 1))
                    nc.vector.tensor_tensor(w_lo[:, 0, k, :], w_raw[:, 0, k, :], w_hi[:, 0, k, :].bitcast(F32),
                                            ALU.subtract).then_inc(first_lo, 1)

            def scale_turn(lay, name):
                kind, i = name
                n = SCALED_TURNS.index(name)
                wait_full(dve, lay, name)
                if lay is not BEFORE:
                    dve.wait_ge(turn_lo, lay * len(SCALED_TURNS) + (n + EARLY_TURNS - 1))
                if kind == "mixed":
                    gain = par[:, PR_PS + 2 * i:PR_PS + 2 * i + 2].unsqueeze(2).to_broadcast([P, 2, SEQ])
                else:
                    first = (PR_MIX if kind == "mix_x" else PR_FFN) + UK * (i // 2)
                    gain = par[:, first:first + UK].unsqueeze(2).to_broadcast([P, UK, P])
                src = turn_view(name, B(name)[:, :])
                dst = turn_view(name, scratch[:, NC * (n % 2):NC * (n % 2) + NC])
                free(nc.vector.tensor_tensor(dst, src, gain, ALU.mult), name)

            def low_turn(lay, name):
                n = HI_TURNS.index(name)
                dve.wait_ge(turn_hi, lay * len(HI_TURNS) + (n + 1 + EARLY_TURNS))
                hi = turn_dest(name, True).bitcast(F32)
                if name[0] in SCALED:
                    k = SCALED_TURNS.index(name)
                    src = scratch[:, NC * (k % 2):NC * (k % 2) + NC]
                    nc.vector.tensor_tensor(turn_dest(name, False), turn_view(name, src), hi, ALU.subtract
                                            ).then_inc(turn_lo, 1)
                else:
                    ins = nc.vector.tensor_tensor(turn_dest(name, False), turn_view(name, B(name)[:, :]), hi,
                                                  ALU.subtract)
                    free(ins, name)

            def turns(lay, names):
                names = [n for n in names if n[0] in SCALED + SPLIT]
                for name in names:
                    if name[0] in SCALED:
                        scale_turn(lay, name)
                for name in names:
                    low_turn(lay, name)

            def rope_tables(lay):
                for k in range(4):
                    axial = k < 2
                    cos, sin = rope_c[:, 0 if axial else 2, :, :], rope_c[:, 1 if axial else 3, :, :]
                    g = par[:, PR_GAIN + HD * k:PR_GAIN + HD * (k + 1)]
                    link(nc.vector.tensor_tensor(rope[:, k, 0, :, :], cos,
                                                 g.unsqueeze(1).to_broadcast([P, MT, HD]), ALU.mult))
                    r = 2 if axial else 1
                    w = HD // (2 * r)
                    for half in range(2):
                        o = rope[:, k, 1, :, :].rearrange("p m (r h w) -> p m r h w", r=r, h=2)[:, :, :, half, :]
                        s = sin.rearrange("p m (r h w) -> p m r h w", r=r, h=2)[:, :, :, half, :]
                        gp = g.rearrange("p (r h w) -> p r h w", r=r, h=2)[:, :, 1 - half, :]
                        link(nc.vector.tensor_tensor(o, s, gp.unsqueeze(1).to_broadcast([P, MT, r, w]), ALU.mult))
                return links[0]

            def rotate(lay, n, region, m, tables):
                name, col, hs, first, k, chunk, _ = region
                W = hs * HD
                z = zqk[:, m, col:col + W]
                t1, t2 = scratch[:, 0:W], scratch[:, B_W:B_W + W]
                wait_emptied(dve, lay, (f"z{chunk}", m))
                if n:
                    dve.wait_ge(rotated, lay * 8 + n)
                else:
                    wait_lo(dve, lay, ("mix_x", 3))
                sq = link(nc.vector.tensor_tensor(t1, z, z, ALU.mult))
                r = 2 if k < 2 else 1
                w = HD // (2 * r)
                after(lay, tables)
                for half in range(2):
                    def part(a, h):
                        return a.rearrange("p (q r h w) -> p q r h w", r=r, h=2, w=w)[:, :, :, h, :]
                    table = rope[:, k, 1, m, :].rearrange("p (r h w) -> p r h w", r=r, h=2)[:, :, half, :]
                    turned = nc.vector.tensor_tensor(part(t2, half), part(z, 1 - half),
                                                     table.unsqueeze(1).to_broadcast([P, hs, r, w]), ALU.mult)
                turned = link(turned)
                after(lay, sq)
                nc.vector.tensor_reduce(ss[:, m, first:first + hs], t1.rearrange("p (h d) -> p h d", d=HD), AX_X,
                                        ALU.add).then_inc(head_sums, 1)
                dve.wait_ge(head_sums, lay * 8 + (n + 1))
                c = link(nc.vector.tensor_tensor(t1.rearrange("p (h d) -> p h d", d=HD),
                                                 z.rearrange("p (h d) -> p h d", d=HD),
                                                 rope[:, k, 0, m, :].unsqueeze(1).to_broadcast([P, hs, HD]),
                                                 ALU.mult))
                after(lay, c)
                s = link(nc.vector.tensor_tensor(t1, t1, t2, ALU.add))
                after(lay, s)
                dve.wait_ge(head_norms, lay * 8 + (n + 1))
                if name == "a_q":
                    dst = z.rearrange("p (j g d) -> p g j d", g=2, d=HD)
                    src = t1.rearrange("p (g j d) -> p g j d", g=2, d=HD)
                    nrm = rs[:, m, first:first + hs].rearrange("p (g j) -> p g j", g=2)
                    for g in range(2):
                        last = nc.vector.tensor_tensor(
                            dst[:, g, :, :], src[:, g, :, :],
                            nrm[:, g, :].unsqueeze(2).to_broadcast([P, 4, HD]), ALU.mult)
                else:
                    last = nc.vector.tensor_tensor(
                        z.rearrange("p (h d) -> p h d", d=HD), t1.rearrange("p (h d) -> p h d", d=HD),
                        rs[:, m, first:first + hs].unsqueeze(2).to_broadcast([P, hs, HD]), ALU.mult)
                last.then_inc(rotated, 1)

            def row_max(lay, i):
                wait_full(dve, lay, ("s", i))
                k = 2 if i < 8 else 1
                nc.vector.tensor_reduce(neg_max[:, 2 * i:2 * i + k],
                                        B(("s", i))[:, :].rearrange("p (h n) -> p h n", h=k), AX_X, ALU.max,
                                        negate=True).then_inc(max_ready, 1)

            def norm_heads(lay, o):
                m, h0, hs = o % 2, (0 if o < 2 else 8), (8 if o < 2 else SLOTS)
                wait_full(dve, lay, ("o", o))
                r = link(nc.vector.reciprocal(rden[:, m, h0:h0 + hs], den[:, m, h0:h0 + hs]))
                after(lay, r)
                free(nc.vector.tensor_tensor(
                    heads[:, m, h0 * HD:(h0 + hs) * HD].rearrange("p (h d) -> p h d", d=HD),
                    B(("o", o))[:, 0:hs * HD].rearrange("p (h d) -> p h d", d=HD),
                    rden[:, m, h0:h0 + hs].unsqueeze(2).to_broadcast([P, hs, HD]), ALU.mult), ("o", o))

            def merge(lay, branch, n, written):
                for m in range(MT):
                    name = ("ABC"[branch] + str(n), m)
                    wait_full(dve, lay, name)
                    if branch == 2:
                        dve.wait_ge(gate_done, lay * 4 + (2 * n + m + 1))
                    gate = gates[:, m, D * branch + NC * n:D * branch + NC * n + NC]
                    to = merged[:, m, NC * n:NC * n + NC]
                    if branch == 2:
                        free(nc.vector.tensor_tensor(to, B(name)[:, :], gate, ALU.mult), name)
                    else:
                        if (branch, n) in ((1, 0), (0, 1)):
                            after(lay, written[(branch, n) == (0, 1)][m])
                        elif (branch, n) == (1, 1):
                            dve.wait_ge(merged_ready, lay * 4 + (m + 1))
                        tmp = scratch[:, NC * m:NC * m + NC]
                        free(nc.vector.tensor_tensor(tmp, B(name)[:, :], gate, ALU.mult), name)
                for m in range(MT):
                    if branch == 2:
                        continue
                    name = ("ABC"[branch] + str(n), m)
                    wait_emptied(dve, lay, name)
                    if written[n][m] is None:
                        wait_emptied(dve, lay, (f"C{n}", m))
                    else:
                        after(lay, written[n][m])
                    to = merged[:, m, NC * n:NC * n + NC]
                    ins = nc.vector.tensor_tensor(to, to, scratch[:, NC * m:NC * m + NC], ALU.add)
                    if written[n][m] is None:
                        written[n][m] = link(ins)
                    else:
                        ins.then_inc(merged_ready, 1)

            def add_x(lay, name, n):
                for m in range(MT):
                    wait_full(dve, lay, (name, m))
                    part = x_sb[:, m, NC * n:NC * n + NC]
                    free(nc.vector.tensor_tensor(part, B((name, m))[:, :], part, ALU.add), (name, m))

            dve.wait_ge(params_loaded, 16)
            turns(BEFORE, [("mix_x", i) for i in range(EARLY_TURNS)])
            dve.wait_ge(mask_loaded, 16)
            nc.vector.tensor_copy(mask_sb[:, P:], gates[:, 0, 0:MT * NC]).then_inc(mask_ready, 1)
            dve.wait_ge(eye_loaded, 16)
            nc.vector.tensor_copy(mask_sb[:, 0:P], ident[:, :]).then_inc(mask_ready, 1)
            dve.wait_ge(angles_loaded, 16)
            dve.wait_ge(x1_loaded, 16)
            with dve.Fori(0, DEPTH) as lay:
                links[0] = 0
                written = [[None] * MT, [None] * MT]
                for t in range(UNITS):
                    if 0 <= t - ATT_STEP < ATT:
                        row_max(lay, t - ATT_STEP)
                    if t in (15, 19, 23, 27):
                        norm_heads(lay, (t - 15) // 4)
                    if t == U_DOWN + 7:
                        dve.wait_ge(params_loaded, lay * 16 + 32)
                    turns(lay, turns_before(t))
                    if t == 0:
                        split_first(lay)
                    for j in splits_at(t):
                        split(lay, j)
                    turns(lay, turns_within(t))
                    if t == 1:
                        tables = rope_tables(lay)
                    for r, region in enumerate(REGIONS):
                        for m in range(MT):
                            if region[-1][m] == t:
                                rotate(lay, 2 * r + m, region, m, tables)
                    c, odd = divmod(t, 2)
                    if odd and GATE_CHUNK <= c < Z_CHUNKS:
                        g = c - GATE_CHUNK
                        dve.wait_ge(bias_loaded[g % 2], lay * 48 + 16 * (g // 2 + 1))
                        for m in range(MT):
                            wait_full(dve, lay, (f"z{c}", m))
                            free(nc.vector.scalar_tensor_tensor(
                                gates[:, m, NC * g:NC * g + NC], B((f"z{c}", m))[:, :], rstd[:, 0, m:m + 1],
                                bias_sb[:, g % 2, :], ALU.mult, ALU.add), (f"z{c}", m))
                    for unit, branch, n in ((U_C0, 2, 0), (U_C1, 2, 1), (U_A0, 0, 0), (U_B, 1, 0), (U_B, 1, 1),
                                            (U_A1, 0, 1)):
                        if t == unit:
                            merge(lay, branch, n, written)
                    if t == U_OUT + 2:
                        add_x(lay, "W0", 0)
                    if t == U_OUT + 3:
                        add_x(lay, "W1", 1)
                    i, odd = divmod(t - U_FFN, 2)
                    if 0 <= i < FC and odd:
                        made = []
                        for m in range(MT):
                            dve.wait_ge(sig_done, lay * 2 * FC + (2 * i + m + 1))
                            made.append(link(nc.vector.scalar_tensor_tensor(
                                scratch[:, 2 * NC + 256 * m:2 * NC + 256 * m + 256], B((f"f{i}", m))[:, 0:256],
                                rstd[:, 1, m:m + 1], sg[:, i % 2, m, :], ALU.mult, ALU.mult)))
                        for m in range(MT):
                            after(lay, made[m])
                            free(nc.vector.scalar_tensor_tensor(
                                hid[:, i % 2, m, :], B((f"f{i}", m))[:, 256:NC], rstd[:, 1, m:m + 1],
                                scratch[:, 2 * NC + 256 * m:2 * NC + 256 * m + 256], ALU.mult, ALU.mult),
                                (f"f{i}", m))
                    if t == U_DOWN + 5:
                        add_x(lay, "D0", 0)
                    if t == U_DOWN + 10:
                        add_x(lay, "D1", 1)
                assert links[0] == VECTOR_LINKS, links[0]

        @block.tensor
        def _(pe):
            pe.sem_inc(unit_done, RING)

            def product(out_ap, hi, lo, slot, k, start, stop, cols=slice(0, NC)):
                nc.tensor.matmul(out_ap, hi, w_lo[:, slot, k, cols], start=start, stop=False)
                nc.tensor.matmul(out_ap, hi, w_hi[:, slot, k, cols], start=False, stop=False)
                return nc.tensor.matmul(out_ap, lo, w_hi[:, slot, k, cols], start=False, stop=stop)

            def unit(lay, t):
                if t:
                    pe.wait_ge(unit_lo, lay * (UNITS - 1) + t)

            def rows(lay, t, name, m, hi, lo, tiles, wk, first, final):
                tok = slice(P * m, P * m + P)
                for i, k in enumerate(tiles):
                    if t == 0 and m == 0:
                        pe.wait_ge(first_lo, lay * UK + (i + 1))
                    last = product(B((name, m))[:, :], hi[:, k, tok], lo[:, k, tok], t % RING, wk + i,
                                   first and i == 0, final and i == len(tiles) - 1)
                if final:
                    full(last, (name, m))
                return last

            def half_unit(lay, t, name, src, tiles, first, final, wk=0):
                for m in range(MT):
                    if m and name != "B1" and name != "D1" or name == "D1" and t > U_DOWN + 5 and m:
                        for turn in turns_within(t):
                            transposes(lay, turn)
                    if first:
                        wait_free(pe, lay, (name, m))
                    last = rows(lay, t, name, m, src[0], src[1], tiles, wk, first, final)
                return last

            def transposes(lay, name):
                kind, i = name
                b = B(name)
                wait_free(pe, lay, name)

                def turn(at, src):
                    return nc.tensor.transpose(b[:, at:at + P], src, ident[:, :])

                if kind in ("mix_x", "ffn_x"):
                    half, m = divmod(i, 2)
                    if kind == "mix_x" and half == 0:
                        if lay is not BEFORE:
                            wait_emptied(pe, lay, ("D0", m))
                    elif kind == "mix_x":
                        pe.wait_ge(bank_free[m], lay * USES[m] + 1)
                    else:
                        wait_emptied(pe, lay, (f"W{half}", m))
                    for k in range(UK):
                        last = turn(P * k, x_sb[:, m, P * (UK * half + k):P * (UK * half + k + 1)])
                elif kind == "merged":
                    half, m = divmod(i, 2)
                    pe.wait_ge(merged_ready, lay * 4 + (i + 1))
                    for k in range(UK):
                        last = turn(P * k, merged[:, m, P * (UK * half + k):P * (UK * half + k + 1)])
                elif kind == "qk":
                    first, k = QK_BATCH[i]
                    region = 0 if i < 2 else 1 if i < 3 else 2 if i < 6 else 3
                    pe.wait_ge(rotated, lay * 8 + 2 * (region + 1))
                    for j in range(k):
                        for m in range(MT):
                            last = turn(P * (2 * j + m), zqk[:, m, P * (first + j):P * (first + j + 1)])
                elif kind == "probs":
                    wait_emptied(pe, lay, ("s", i))
                    for c in range(4):
                        last = turn(P * c, probs[:, i % 2, P * c:P * c + P])
                elif kind == "heads":
                    wait_emptied(pe, lay, ("o", i))
                    m, c0, k = i % 2, (0 if i < 2 else A_Q), (4 if i < 2 else 2)
                    for c in range(k):
                        last = turn(P * c, heads[:, m, c0 + P * c:c0 + P * c + P])
                elif kind == "hidden":
                    for m in range(MT):
                        wait_emptied(pe, lay, (f"f{i}", m))
                    for k in range(2):
                        for m in range(MT):
                            last = turn(P * (2 * k + m), hid[:, i % 2, m, P * k:P * k + P])
                elif kind == "pool":
                    if i == 0:
                        pe.wait_ge(pooling_loaded, 16)
                        for m in range(MT):
                            wait_emptied(pe, lay, (f"z{POOL_CHUNK}", m))
                    for g in (2 * i, 2 * i + 1):
                        for m in range(MT):
                            last = nc.tensor.matmul(b[:, SEQ * (g % 2):SEQ * (g % 2) + SEQ],
                                                    zvu[:, m, VU_POOL + P * g:VU_POOL + P * g + P],
                                                    pool_mat[:, m, g, :], start=(m == 0), stop=(m == MT - 1))
                else:
                    wait_emptied(pe, lay, ("pool", i))
                    for g in (2 * i, 2 * i + 1):
                        last = nc.tensor.matmul(b[:, SEQ * (g % 2):SEQ * (g % 2) + SEQ], lin[:, g, :],
                                                pooledT[:, g, :], start=True, stop=True)
                full(last, name)

            def scores(lay, i):
                wait_free(pe, lay, ("s", i))
                b = B(("s", i))
                if i == 0:
                    wait_emptied(pe, lay, ("qk", 2))
                if i == 8:
                    pe.wait_ge(mask_ready, 2)
                    wait_emptied(pe, lay, ("qk", 7))
                    wait_emptied(pe, lay, ("qk", 8))
                if i < 8:
                    m, (g, pair) = i // 4, divmod(i % 4, 2)
                    part = slice(HD * g, HD * g + HD)
                    for hh in range(2):
                        last = nc.tensor.matmul(b[:, SEQ * hh:SEQ * hh + SEQ],
                                                qkT[part, QT_A_Q + 2 * pair + hh, P * m:P * m + P],
                                                qkT[part, QT_A_K, :], start=True, stop=True)
                else:
                    m, s = (i - 8) // 4, i % 4
                    nc.tensor.matmul(b[:, :], ident_b, mask_m[m], start=True, stop=False)
                    part = slice(HD * (s % 2), HD * (s % 2) + HD)
                    for g in range(GROUPS):
                        tile = 2 * g + s // 2
                        cols, keys = (slice(0, SEQ), slice(0, SEQ)) if g == 0 else \
                            (slice(SEQ + P * (g - 1), SEQ + P * g), slice(P * m, P * m + P))
                        last = nc.tensor.matmul(b[:, cols], qkT[part, QT_B_Q + tile, P * m:P * m + P],
                                                qkT[part, QT_B_K + tile, keys], start=False,
                                                stop=(g == GROUPS - 1))
                full(last, ("s", i))

            def values(lay, i):
                wait_emptied(pe, lay, ("probs", i))
                if i < 8:
                    m, h, o = i // 4, 2 * (i % 4), i // 4
                    todo = [(h + hh, [(2 * hh + kt, kt, VU_A + HD * ((h + hh) // 4)) for kt in range(MT)])
                            for hh in range(2)]
                else:
                    m, s, o = (i - 8) // 4, i % 4, 2 + (i - 8) // 4
                    v = [VU_B + HD * (SLOTS * g + s) for g in range(GROUPS)]
                    todo = [(s, [(0, 0, v[0]), (1, 1, v[0]), (2, m, v[1]), (3, m, v[2])])]
                if i % 4 == 0:
                    wait_free(pe, lay, ("o", o))
                for h, terms in todo:
                    for n, (c, kt, col) in enumerate(terms):
                        last = nc.tensor.matmul(B(("o", o))[:, HD * h:HD * h + HD],
                                                probsT[:, i % 2, P * c:P * c + P], zvu[:, kt, col:col + HD],
                                                start=(n == 0), stop=(n == len(terms) - 1))
                if i % 4 == 3:
                    full(last, ("o", o))

            aT, oT, mixT, hT = (aT_hi, aT_lo), (oT_hi, oT_lo), (mixT_hi, mixT_lo), (hT_hi, hT_lo)
            pe.wait_ge(x0_loaded, 16)
            pe.wait_ge(eye_loaded, 16)
            for i in range(EARLY_TURNS):
                transposes(BEFORE, ("mix_x", i))
            pe.wait_ge(x1_loaded, 16)
            with pe.Fori(0, DEPTH) as lay:
                for t in range(UNITS):
                    for name in turns_before(t):
                        if name[0] == "probs":
                            transposes(lay, name)
                    if 0 <= t - ATT_STEP < ATT:
                        scores(lay, t - ATT_STEP)
                    if 0 <= t - ATT_STEP - 3 < ATT:
                        values(lay, t - ATT_STEP - 3)
                    for name in turns_before(t):
                        if name[0] != "probs":
                            transposes(lay, name)
                    unit(lay, t)
                    if t < U_C0:
                        c, half = divmod(t, 2)
                        if c == 0:
                            for m in range(MT):
                                wait_lo(pe, lay, ("mix_x", 2 * half + m), former=half == 0)
                        last = half_unit(lay, t, f"z{c}", aT, range(UK * half, UK * half + UK), half == 0, half == 1)
                    elif t in (U_C0, U_C1):
                        if t == U_C0:
                            for i in range(2):
                                wait_lo(pe, lay, ("mixed", i))
                        last = half_unit(lay, t, f"C{t - U_C0}", mixT, range(4), True, True)
                    elif t in (U_A0, U_A1):
                        if t == U_A0:
                            wait_emptied(pe, lay, ("heads", 0))
                            wait_emptied(pe, lay, ("heads", 1))
                        last = half_unit(lay, t, "A0" if t == U_A0 else "A1", oT, range(4), True, True)
                    elif t == U_B:
                        wait_emptied(pe, lay, ("heads", 2))
                        wait_emptied(pe, lay, ("heads", 3))
                        half_unit(lay, t, "B0", oT, (4, 5), True, True)
                        last = half_unit(lay, t, "B1", oT, (4, 5), True, True, wk=2)
                    elif t < U_FFN:
                        half, n = divmod(t - U_OUT, 2)
                        if n == 0:
                            for m in range(MT):
                                wait_emptied(pe, lay, ("merged", 2 * half + m))
                        last = half_unit(lay, t, f"W{n}", aT, range(UK * half, UK * half + UK), half == 0, half == 1)
                    elif t < U_DOWN:
                        i, half = divmod(t - U_FFN, 2)
                        if i == 0:
                            for m in range(MT):
                                wait_lo(pe, lay, ("ffn_x", 2 * half + m))
                        last = half_unit(lay, t, f"f{i}", aT, range(UK * half, UK * half + UK), half == 0, half == 1)
                    else:
                        q = t - U_DOWN
                        if q < 5:
                            for i in (2 * q, 2 * q + 1):
                                wait_emptied(pe, lay, ("hidden", i))
                            last = half_unit(lay, t, "D0", hT, range(UK * q, UK * q + UK), q == 0, False)
                        elif q == 5:
                            wait_emptied(pe, lay, ("hidden", FC - 1))
                            half_unit(lay, t, "D0", hT, (20, 21), False, True)
                            last = half_unit(lay, t, "D1", hT, (20, 21), True, False, wk=2)
                        else:
                            q -= 6
                            last = half_unit(lay, t, "D1", hT, range(UK * q, UK * q + UK), False, q == 4)
                    last.then_inc(unit_done, 1)


def constants():
    import numpy as np
    tok = np.stack([2 * np.arange(P) + m for m in range(MT)])
    flat = tok.reshape(-1)

    def angles(pos, dim):
        inv = np.float32(10000.0) ** (-np.arange(0, dim, 2, dtype=np.float32) / np.float32(dim))
        return (pos.astype(np.float32)[..., None] * inv.astype(np.float32)).astype(np.float32)

    def table(parts):
        cos = np.concatenate([np.concatenate([np.cos(a), np.cos(a)], -1) for a in parts], -1)
        sin = np.concatenate([np.concatenate([-np.sin(a), np.sin(a)], -1) for a in parts], -1)
        return cos, sin

    axial = table([angles(tok // 64, HD // 2), angles(tok % 64, HD // 2)])
    plain = table([angles(tok, HD)])
    rope = np.stack([axial[0], axial[1], plain[0], plain[1]])
    pool = np.zeros((SEQ, POOL_G, SEQ), np.float32)
    for g, w in enumerate((2, 4, 8, 16)):
        for n, t in enumerate(flat):
            lo, hi = max(t - w // 2, 0), min(t + w - w // 2, SEQ)
            inside = (flat >= lo) & (flat < hi)
            pool[inside, g, n] = np.float32(1.0) / np.float32(hi - lo)
            pool[n, g, n] -= np.float32(1.0)
    eye = np.eye(P, dtype=np.float32)
    rope = np.ascontiguousarray(rope.transpose(2, 0, 1, 3).reshape(P, -1), np.float32)
    pool = np.ascontiguousarray(pool.reshape(MT, P, POOL_G, SEQ).transpose(1, 0, 2, 3).reshape(P, -1))
    masks = []
    for m in range(MT):
        q = tok[m][:, None]
        masks.append(np.concatenate([
            np.where(np.abs(q - flat[None, :]) <= 64, 0.0, NEG_INF),
            np.where((q - tok[m][None, :]) % 4 == 0, 0.0, NEG_INF),
            np.where((q - tok[m][None, :]) % 16 == 0, 0.0, NEG_INF)], 1))
    return {"eye": eye, "angles": rope, "pooling": pool, "mask": np.concatenate(masks, 1).astype(np.float32)}


def weight_stream(w_in, w_branch_a, w_branch_b, w_branch_c, w_out, w_ffn_gate, w_ffn_up, w_ffn_down):
    import numpy as np
    units = np.empty((DEPTH, UNITS, P, UK, NC), np.float32)
    for l in range(DEPTH):
        u = units[l]
        w = w_in[l].reshape(2, UK, P, Z_CHUNKS, NC)
        u[:U_C0] = w.transpose(3, 0, 2, 1, 4).reshape(2 * Z_CHUNKS, P, UK, NC)
        c = w_branch_c[l].reshape(UK, P, 2, NC)
        a = w_branch_a[l].reshape(UK, P, 2, NC)
        for n, (uc, ua) in enumerate(((U_C0, U_A0), (U_C1, U_A1))):
            u[uc] = c[:, :, n].transpose(1, 0, 2)
            u[ua] = a[:, :, n].transpose(1, 0, 2)
        b = w_branch_b[l].reshape(2, P, 2, NC)
        u[U_B] = b.transpose(1, 2, 0, 3).reshape(P, UK, NC)
        w = w_out[l].reshape(2, UK, P, 2, NC)
        u[U_OUT:U_FFN] = w.transpose(0, 3, 2, 1, 4).reshape(4, P, UK, NC)
        for at, w in ((0, w_ffn_gate[l]), (256, w_ffn_up[l])):
            w = w.reshape(2, UK, P, FC, 256).transpose(3, 0, 2, 1, 4)
            u[U_FFN:U_DOWN, :, :, at:at + 256] = w.reshape(2 * FC, P, UK, 256)
        w = w_ffn_down[l].reshape(KF, P, 2, NC)
        for n, first in ((0, U_DOWN), (1, U_DOWN + 6)):
            u[first:first + 5] = w[:20, :, n].reshape(5, UK, P, NC).transpose(0, 2, 1, 3)
        u[U_DOWN + 5] = w[20:].transpose(1, 2, 0, 3).reshape(P, UK, NC)
    return units.reshape(DEPTH * UNITS, P, UNIT)


def layer_params(norm_mix, norm_ffn, pool_scale, qn_a, kn_a, qn_b, kn_b, pool_lin):
    import numpy as np
    par = np.empty((DEPTH, P, PR_W), np.float32)
    par[:, :, PR_MIX:PR_MIX + KT] = norm_mix.reshape(DEPTH, KT, P).transpose(0, 2, 1)
    par[:, :, PR_FFN:PR_FFN + KT] = norm_ffn.reshape(DEPTH, KT, P).transpose(0, 2, 1)
    par[:, :, PR_PS:PR_PS + POOL_G] = pool_scale.reshape(DEPTH, POOL_G, P).transpose(0, 2, 1)
    for k, g in enumerate((qn_a, kn_a, qn_b, kn_b)):
        par[:, :, PR_GAIN + HD * k:PR_GAIN + HD * (k + 1)] = g[:, None, :]
    par[:, :, PR_LIN:] = pool_lin.transpose(0, 2, 1, 3).reshape(DEPTH, P, POOL_G * P)
    return par


def kernel(**inputs):
    import numpy as np
    import concourse.bacc as bacc
    from concourse.bass_utils import run_bass_kernel_spmd

    i = {k: np.asarray(v) for k, v in inputs.items()}
    host = {
        "x": np.ascontiguousarray(i["x"]),
        "stream": weight_stream(i["w_in"], i["w_branch_a"], i["w_branch_b"], i["w_branch_c"], i["w_out"],
                                i["w_ffn_gate"], i["w_ffn_up"], i["w_ffn_down"]),
        "params": layer_params(i["norm_mix"], i["norm_ffn"], i["pool_scale"], i["qn_a"], i["kn_a"], i["qn_b"],
                               i["kn_b"], i["pool_lin"]),
        "b_gate": np.ascontiguousarray(i["b_gate"].reshape(DEPTH, 3 * D // NC, NC)),
        **constants(),
    }
    nc = bacc.Bacc("TRN2", target_bir_lowering=False, num_devices=1, dynamic_dma_scratch_size=4096)
    arrays, args = {}, []
    for name, a in host.items():
        arrays[f"in_{name}_dram"] = a
        args.append(nc.dram_tensor(f"in_{name}_dram", a.shape, mybir.dt.from_np(a.dtype), kind="ExternalInput").ap())
    args.append(nc.dram_tensor("out_0_dram", (1, SEQ, D), F32, kind="ExternalOutput").ap())
    build(nc, *args)
    r = run_bass_kernel_spmd(nc, [arrays], core_ids=[0])
    return r.results[0]["out_0_dram"]
```

```python
from contextlib import ExitStack

import concourse.bass as bass
from concourse import mybir

F32 = mybir.dt.float32
F32R = mybir.dt.float32r
BF16 = mybir.dt.bfloat16
ALU = mybir.AluOpType
ACT = mybir.ActivationFunctionType
AX_X = mybir.AxisListType.X

P = 128
DEPTH, SEQ, D = 2, 256, 1024
HD = 64
EPS = 1e-6
NEG_INF = -1e30
MT = SEQ // P
KT = D // P
NC = 512
UK = 4
UNIT = UK * NC
D_FF = 2816
A_Q, A_KV, B_W, POOL_W = 512, 128, 768, 512
GROUPS, SLOTS = 3, 4
POOL_G = 4
Z_CHUNKS, GATE_CHUNK, POOL_CHUNK = 13, 7, 6
FC = D_FF // 256
KF = D_FF // P
RING = 4

U_Z = 0
U_C0, U_C1, U_A0, U_B, U_A1 = 26, 27, 28, 29, 30
U_OUT = 31
U_FFN = 35
U_DOWN = U_FFN + 2 * FC
UNITS = U_DOWN + 11
assert UNITS % RING == 0

QK_A_Q, QK_A_K, QK_B_Q, QK_B_K = 0, 512, 640, 1408
QK_W = 2176
VU_A, VU_B, VU_POOL = 0, 128, 896
VU_W = 1408
Z_PIECES = [
    [(0, 512, "qk", 0)],
    [(0, 128, "qk", 512), (128, 128, "vu", 0), (256, 256, "qk", 640)],
    [(0, 512, "qk", 896)],
    [(0, 512, "qk", 1408)],
    [(0, 256, "qk", 1920), (256, 256, "vu", 128)],
    [(0, 512, "vu", 384)],
    [(0, 512, "vu", 896)],
]
REGIONS = [
    ("a_q", QK_A_Q, 8, 0, 0, 0, (2, 3)),
    ("a_k", QK_A_K, 2, 8, 1, 1, (4, 4)),
    ("b_q0", QK_B_Q, 4, 10, 2, 1, (5, 5)),
    ("b_q1", QK_B_Q + 4 * HD, 8, 14, 2, 2, (6, 7)),
    ("b_k0", QK_B_K, 8, 22, 3, 3, (8, 9)),
    ("b_k1", QK_B_K + 8 * HD, 4, 30, 3, 4, (10, 11)),
]
HEADS = 34
TURNED = len(REGIONS) * MT
QT_A_Q, QT_A_K, QT_B_Q, QT_B_K, QTILES = 0, 4, 5, 11, 17

PR_MIX, PR_FFN, PR_PS, PR_GAIN, PR_LIN = 0, 8, 16, 20, 20 + 4 * HD
PR_W = PR_LIN + POOL_G * P

ATT = 16
ATT_STEP = 9

TURNS_BEFORE = {
    6: [("qk", 0)], 7: [("qk", 2)], 14: [("qk", 6)], 28: [("heads", 3)],
    32: [("merged", 2), ("merged", 3)],
    U_DOWN + 7: [("mix_x", 0), ("mix_x", 1)],
}
TURNS_WITHIN = {
    0: [("mix_x", 2), ("mix_x", 3)], 6: [("qk", 1)],
    10: [("qk", 3)], 11: [("qk", 4)], 12: [("qk", 5)], 14: [("qk", 7)], 15: [("qk", 8)],
    16: [("heads", 0)], 17: [("pool", 0)], 18: [("pool", 1)], 20: [("mixed", 0)], 21: [("mixed", 1)],
    22: [("heads", 1)], 25: [("heads", 2)], 30: [("merged", 0), ("merged", 1)],
    U_OUT + 3: [("ffn_x", 0), ("ffn_x", 1)], U_FFN: [("ffn_x", 2), ("ffn_x", 3)],
}


TURNS_FIRST = (0, U_A1, U_OUT + 3, U_FFN)


def turns_before(t):
    out = []
    if 0 <= t - ATT_STEP - 2 < ATT:
        out.append(("probs", t - ATT_STEP - 2))
    out += TURNS_BEFORE.get(t, [])
    i, odd = divmod(t - U_FFN - 3, 2)
    if 0 <= i < FC and not odd:
        out.append(("hidden", i))
    return out


def turns_within(t):
    return TURNS_WITHIN.get(t, [])


QK_BATCH = [(0, 2), (2, 2), (4, 1), (5, 2), (7, 2), (9, 2), (11, 2), (13, 2), (15, 2)]
SCALED = ("mix_x", "mixed", "ffn_x")
SPLIT = ("heads", "merged", "hidden")
PLAIN = ("qk", "probs", "pool")


X_BANKS = (4, 0)


def plan_banks():
    order = {b: [] for b in range(8)}

    def pair(first, name):
        for m in range(MT):
            order[first + m].append((name, m))

    for c in range(Z_CHUNKS):
        pair(2 if c in (0, 2, 4) else 0, f"z{c}")
    order[2] += [("o", 0), ("o", 2)]
    order[3] += [("o", 1), ("o", 3)]
    for i in range(ATT):
        order[4 + i % 2].append(("s", i))
    for first, name in ((4, "C0"), (0, "C1"), (4, "A0"), (2, "B0"), (0, "B1"), (4, "A1"), (2, "W0"), (0, "W1")):
        pair(first, name)
    for i in range(FC):
        pair(2 * ((i + 1) % 2), f"f{i}")
    pair(X_BANKS[0], "D0")
    pair(X_BANKS[1], "D1")
    n = 0
    for t in range(UNITS):
        for b in turns_before(t) + turns_within(t):
            order[6 + n % 2].append(b)
            n += 1
    assert n % 2 == 0
    use = {name: (b, k) for b, names in order.items() for k, name in enumerate(names)}
    return order, use, {b: len(names) for b, names in order.items()}


ORDER, USE, USES = plan_banks()

UNIT_ENDS = {(f"z{c}", 1): 2 * c + 1 for c in range(Z_CHUNKS)}
UNIT_ENDS |= {("C0", 1): U_C0, ("C1", 1): U_C1, ("A0", 1): U_A0, ("B1", 1): U_B, ("A1", 1): U_A1,
              ("W0", 1): U_OUT + 2, ("W1", 1): U_OUT + 3, ("D1", 1): U_DOWN + 10}
UNIT_ENDS |= {(f"f{i}", 1): U_FFN + 2 * i + 1 for i in range(FC)}
FULL = {name: n for b in ORDER for n, name in enumerate([x for x in ORDER[b] if x not in UNIT_ENDS])}
FULLS = {b: len([x for x in names if x not in UNIT_ENDS]) for b, names in ORDER.items()}

HI_TURNS = [b for t in range(UNITS) for b in turns_before(t) + turns_within(t) if b[0] in SCALED + SPLIT]
SCALED_TURNS = [b for b in HI_TURNS if b[0] in SCALED]
EARLY = {b: int(b >= 6) for b in range(8)}
EARLY_TURNS = 2
BEFORE = -1
VECTOR_LINKS = 12 + TURNED * 3 + 4 + 2 * MT + MT * FC
POOL_LINKS = 4 + TURNED


def splits_at(t, ahead=2):
    if t < 2:
        return {2: ([1], [2, 3]), 3: ([1, 2], [3])}[ahead][t]
    return [t + 2] if t + 2 < UNITS else []


def build(nc, x, stream, params, b_gate, eye, angles, pooling, mask, out):
    stream_v = stream.rearrange("u p n -> (u p) n")
    params_v = params.rearrange("l p n -> (l p) n")
    gate_v = b_gate.rearrange("l g n -> (l g) n")
    with ExitStack() as ctx:
        def sb(name, shape, dt=F32, to=ctx):
            return to.enter_context(nc.sbuf_tensor(name, shape, dt))

        def sem(name):
            return ctx.enter_context(nc.semaphore(name))

        w_hi = sb("w_hi", [P, RING, UK, NC], F32R)
        with ExitStack() as shared:
            w_raw = sb("w_raw", [P, RING, UK, NC], F32, shared)
        w_lo = sb("w_lo", [P, RING, UK, NC], F32R)
        x_sb = sb("x_sb", [P, MT, D])
        aT_hi = sb("aT_hi", [P, KT, SEQ], F32R)
        aT_lo = sb("aT_lo", [P, KT, SEQ], F32R)
        qkT = sb("qkT", [P, QTILES, SEQ])
        probs = sb("probs", [P, 2, NC])
        probsT = sb("probsT", [P, 2, NC])
        scratch = sb("scratch", [P, 3 * NC])
        bias_sb = sb("bias_sb", [P, 2, NC])
        ident = sb("ident", [P, P])
        rope_c = sb("rope_c", [P, 4, MT, HD])
        pool_mat = sb("pool_mat", [P, MT, POOL_G, SEQ])
        mask_sb = sb("mask_sb", [P, P + MT * NC], BF16)
        rope = sb("rope", [P, 4, 2, MT, HD])
        par = sb("par", [P, PR_W])
        mixT_hi = sb("mixT_hi", [P, POOL_G, SEQ], F32R)
        mixT_lo = sb("mixT_lo", [P, POOL_G, SEQ], F32R)
        oT_hi = sb("oT_hi", [P, 6, SEQ], F32R)
        oT_lo = sb("oT_lo", [P, 6, SEQ], F32R)
        ss = sb("ss", [P, MT, HEADS])
        rs = sb("rs", [P, MT, HEADS])
        rs_in = sb("rs_in", [P, MT, HEADS])
        neg_half = sb("neg_half", [P, MT, HEADS])
        ssx = sb("ssx", [P, 2, MT])
        sx = sb("sx", [P, 2, MT])
        rstd = sb("rstd", [P, 2, MT])
        table_warm = sb("table_warm", [P, MT])
        neg_max = sb("neg_max", [P, 2 * ATT])
        den = sb("den", [P, MT, 8 + SLOTS])
        rden = sb("rden", [P, MT, 8 + SLOTS])
        with ExitStack() as mixer:
            with ExitStack() as early:
                zqk = sb("zqk", [P, MT, QK_W], F32, early)
            with ExitStack() as late:
                merged = sb("merged", [P, MT, D], F32, late)
                sb("late_gap", [P, QK_W - MT * D], F32, late)
                heads = sb("heads", [P, MT, A_Q + SLOTS * HD], F32, late)
                pooledT = sb("pooledT", [P, POOL_G, SEQ], F32, late)
            sb("late_room", [P, MT * (A_Q + SLOTS * HD) + QK_W + POOL_G * SEQ], F32, mixer)
            zvu = sb("zvu", [P, MT, VU_W], F32, mixer)
            gates = sb("gates", [P, MT, 3 * D], F32, mixer)
        hT_hi = sb("hT_hi", [P, KF, SEQ], F32R)
        hT_lo = sb("hT_lo", [P, KF, SEQ], F32R)
        sg = sb("sg", [P, 2, MT, 256])
        hid = sb("hid", [P, 2, MT, 256])

        squares = gates[:, :, 0:QK_W]
        mask_f = gates[:, 1, D * 2:D * 2 + MT * NC]
        ident_b = mask_sb[:, 0:P]
        mask_m = [mask_sb[:, P + m * NC:P + (m + 1) * NC] for m in range(MT)]
        lin = par[:, PR_LIN:PR_W].rearrange("p (g d) -> p g d", g=POOL_G)
        gate_v3 = gates[:, :, :].rearrange("p m (b n c) -> p m b n c", b=3, n=2)

        bank = [ctx.enter_context(nc.psum_tensor(f"bank{b}", [P, NC], F32)) for b in range(8)]

        x0_loaded = sem("x0_loaded")
        x1_loaded = sem("x1_loaded")
        eye_loaded = sem("eye_loaded")
        angles_loaded = sem("angles_loaded")
        pooling_loaded = sem("pooling_loaded")
        mask_loaded = sem("mask_loaded")
        mask_ready = sem("mask_ready")
        gains_loaded = sem("gains_loaded")
        params_loaded = sem("params_loaded")
        bias_loaded = [sem(f"bias_loaded{i}") for i in range(2)]
        unit_landed = [sem(f"unit_landed{i}") for i in range(RING)]
        unit_done = sem("unit_done")
        unit_hi = sem("unit_hi")
        unit_lo = sem("unit_lo")
        first_hi = sem("first_hi")
        first_lo = sem("first_lo")
        bank_full = [sem(f"bank_full{b}") for b in range(8)]
        bank_free = [sem(f"bank_free{b}") for b in range(8)]
        turn_hi = sem("turn_hi")
        turn_lo = sem("turn_lo")
        half_ready = sem("half_ready")
        head_sums = sem("head_sums")
        head_norms = sem("head_norms")
        rotated = sem("rotated")
        x_sums = sem("x_sums")
        x_norm = sem("x_norm")
        max_ready = sem("max_ready")
        gate_done = sem("gate_done")
        merged_ready = sem("merged_ready")
        sig_done = sem("sig_done")
        vchain = sem("vchain")
        pchain = sem("pchain")
        out_done = sem("out_done")

        def B(name):
            return bank[USE[name][0]]

        def wait_free(eng, lay, name):
            b, k = USE[name]
            eng.wait_ge(bank_free[b], lay * USES[b] + (k + 1 + EARLY[b]))

        def wait_full(eng, lay, name):
            if name in UNIT_ENDS:
                eng.wait_ge(unit_done, lay * UNITS + (RING + UNIT_ENDS[name] + 1))
            else:
                b = USE[name][0]
                eng.wait_ge(bank_full[b], lay * FULLS[b] + (FULL[name] + 1 + EARLY[b]))

        def wait_emptied(eng, lay, name):
            b, k = USE[name]
            eng.wait_ge(bank_free[b], lay * USES[b] + (k + 2 + EARLY[b]))

        def full(ins, name):
            if name not in UNIT_ENDS:
                ins.then_inc(bank_full[USE[name][0]], 1)

        def free(ins, name):
            ins.then_inc(bank_free[USE[name][0]], 1)

        def wait_lo(eng, lay, name, former=False):
            n = SCALED_TURNS.index(name) + 1 + EARLY_TURNS - (len(SCALED_TURNS) if former else 0)
            eng.wait_ge(turn_lo, lay * len(SCALED_TURNS) + n)

        def turn_dest(name, hi):
            kind, i = name
            if kind in ("mix_x", "merged", "ffn_x"):
                to = aT_hi if hi else aT_lo
                return to[:, UK * (i // 2):UK * (i // 2) + UK, P * (i % 2):P * (i % 2) + P]
            if kind == "mixed":
                return (mixT_hi if hi else mixT_lo)[:, 2 * i:2 * i + 2, :]
            if kind == "heads":
                to, m = (oT_hi if hi else oT_lo), i % 2
                return to[:, 0:4, m * P:m * P + P] if i < 2 else to[:, 4:6, m * P:m * P + P]
            to = hT_hi if hi else hT_lo
            return to[:, 2 * i:2 * i + 2, :]

        def turn_view(name, ap):
            kind, i = name
            if kind in ("mix_x", "merged", "ffn_x"):
                return ap.rearrange("p (k n) -> p k n", k=UK)
            if kind == "heads":
                return ap.rearrange("p (k n) -> p k n", k=4) if i < 2 else \
                    ap[:, 0:2 * P].rearrange("p (k n) -> p k n", k=2)
            return ap.rearrange("p (k n) -> p k n", k=2)

        block = ctx.enter_context(nc.Block())

        xv = x.rearrange("b (p m) d -> (b p) m d", m=MT)

        @block.sync
        def _(sp):
            sp.dma_start(x_sb[:, :, 0:NC], xv[:, :, 0:NC]).then_inc(x0_loaded, 16)
            sp.dma_start(ident[:, :], eye).then_inc(eye_loaded, 16)
            with sp.Fori(0, DEPTH * UNITS // RING) as turn:
                for s in range(RING):
                    sp.wait_ge(unit_done, turn * RING + (s + 1))
                    sp.dma_start(w_raw[:, s, :, :].rearrange("p k n -> p (k n)"),
                                 stream_v[bass.ds((turn * RING + s) * P, P), :]
                                 ).then_inc(unit_landed[s], 16)
            ov = out.rearrange("b (p m) d -> (b p) m d", m=MT)
            for half, first in enumerate(X_BANKS):
                for m in range(MT):
                    sp.wait_ge(bank_free[first + m], DEPTH * USES[first + m] + 1)
                    cols = slice(NC * half, NC * half + NC)
                    sp.dma_start(ov[:, m, cols], x_sb[:, m, cols]).then_inc(out_done, 16)
            sp.wait_ge(out_done, 16 * 2 * MT)

        @block.gpsimd
        def _(pool):
            def load_gains(layer):
                pool.dma_start(par[:, 0:PR_GAIN], params_v[layer * P:layer * P + P, 0:PR_GAIN]
                               ).then_inc(gains_loaded, 16)

            def load_params(layer):
                pool.dma_start(par[:, PR_GAIN:PR_W], params_v[layer * P:layer * P + P, PR_GAIN:PR_W]
                               ).then_inc(params_loaded, 16)

            nc.gpsimd.memset(neg_half[:, :, :], -0.5).then_inc(half_ready, 1)
            load_gains(0)
            pool.dma_start(x_sb[:, :, NC:D], xv[:, :, NC:D]).then_inc(x1_loaded, 16)
            load_params(0)
            pool.dma_start(rope_c[:, :, :, :].rearrange("p k m d -> p (k m d)"), angles
                           ).then_inc(angles_loaded, 16)
            pool.dma_start(mask_f, mask).then_inc(mask_loaded, 16)
            pool.wait_ge(half_ready, 1)

            def power(lay, link, dst, src, mul, eps, signal):
                nc.gpsimd.tensor_scalar(dst[1], src, mul, eps, ALU.mult, ALU.add).then_inc(pchain, 1)
                pool.wait_ge(pchain, lay * POOL_LINKS + (link + 1))
                nc.gpsimd.tensor_tensor(dst[0], dst[1], dst[2], ALU.pow).then_inc(signal, 1)

            def x_norms(lay, which, link):
                pool.wait_ge(x_sums, lay * 8 + 4 * (which + 1))
                nc.gpsimd.tensor_tensor(sx[:, which, :], ssx[:, 0, :], ssx[:, 1, :], ALU.add
                                        ).then_inc(pchain, 1)
                pool.wait_ge(pchain, lay * POOL_LINKS + (link + 1))
                power(lay, link + 1, (rstd[:, which, :], sx[:, which, :], neg_half[:, 0, 0:MT]),
                      sx[:, which, :], 1.0 / D, EPS, x_norm)

            def load_bias(lay, g):
                if g >= 2:
                    for m in range(MT):
                        wait_emptied(pool, lay, (f"z{GATE_CHUNK + g - 2}", m))
                pool.dma_start(bias_sb[:, g % 2, :],
                               gate_v[lay * 6 + g:lay * 6 + g + 1, :].to_broadcast([P, NC])
                               ).then_inc(bias_loaded[g % 2], 16)

            for lay in range(DEPTH):
                load_bias(lay, 0)
                load_bias(lay, 1)
                if lay == 0:
                    pool.wait_ge(eye_loaded, 16)
                    nc.gpsimd.tensor_copy(mask_sb[:, 0:P], ident[:, :]).then_inc(mask_ready, 1)
                    pool.wait_ge(mask_loaded, 16)
                    nc.gpsimd.tensor_copy(mask_sb[:, P:], mask_f).then_inc(mask_ready, 1)
                x_norms(lay, 0, 0)
                if lay == 0:
                    pool.dma_start(pool_mat[:, :, :, :].rearrange("p m g n -> p (m g n)"), pooling
                                   ).then_inc(pooling_loaded, 16)
                n = 0
                for name, _, hs, first, _, _, _ in REGIONS:
                    mul, eps = (1.0, HD * EPS) if name[2] == "q" else (1.0 / HD, EPS)
                    for m in range(MT):
                        pool.wait_ge(head_sums, lay * TURNED + (n + 1))
                        h = slice(first, first + hs)
                        power(lay, 2 + n, (rs[:, m, h], rs_in[:, m, h], neg_half[:, m, h]),
                              ss[:, m, h], mul, eps, head_norms)
                        n += 1
                for g in range(2, 6):
                    load_bias(lay, g)
                x_norms(lay, 1, 2 + TURNED)
                wait_lo(pool, lay, ("ffn_x", 3))
                load_gains(min(lay + 1, DEPTH - 1))
                load_params(min(lay + 1, DEPTH - 1))

        @block.scalar
        def _(act):
            for b in range(0, 8):
                act.sem_inc(bank_free[b], 1)

            def split_first(lay):
                act.wait_ge(unit_landed[0], lay * (16 * UNITS // RING) + 16)
                for k in range(UK):
                    nc.scalar.activation(w_hi[:, 0, k, :], w_raw[:, 0, k, :], ACT.Copy).then_inc(first_hi, 1)

            def split(lay, j):
                act.wait_ge(unit_landed[j % RING], lay * (16 * UNITS // RING) + 16 * (j // RING + 1))
                nc.scalar.activation(w_hi[:, j % RING, :, :].rearrange("p k n -> p (k n)"),
                                     w_raw[:, j % RING, :, :].rearrange("p k n -> p (k n)"),
                                     ACT.Copy).then_inc(unit_hi, 1)

            def turn(lay, name):
                kind, i = name
                if kind in SCALED:
                    n = SCALED_TURNS.index(name)
                    wait_emptied(act, lay, name)
                    src = scratch[:, NC * (n % 2):NC * (n % 2) + NC]
                    nc.scalar.activation(turn_dest(name, True), turn_view(name, src), ACT.Copy
                                         ).then_inc(turn_hi, 1)
                    return
                wait_full(act, lay, name)
                if kind in SPLIT:
                    nc.scalar.activation(turn_dest(name, True), turn_view(name, B(name)[:, :]), ACT.Copy
                                         ).then_inc(turn_hi, 1)
                elif kind == "qk":
                    first, k = QK_BATCH[i]
                    free(nc.scalar.activation(qkT[:, first:first + k, :].rearrange("p k n -> p (k n)"),
                                              B(name)[:, 0:k * SEQ], ACT.Copy), name)
                elif kind == "probs":
                    free(nc.scalar.activation(probsT[:, i % 2, :], B(name)[:, :], ACT.Copy), name)
                else:
                    free(nc.scalar.activation(pooledT[:, 2 * i:2 * i + 2, :].rearrange("p k n -> p (k n)"),
                                              B(name)[:, :], ACT.Copy), name)

            def softmax_exp(lay, i):
                act.wait_ge(max_ready, lay * ATT + (i + 1))
                if i < 8:
                    m, h = i // 4, 2 * (i % 4)
                    nc.scalar.activation(probs[:, i % 2, 0:SEQ], B(("s", i))[:, 0:SEQ], ACT.Exp,
                                         bias=neg_max[:, 2 * i:2 * i + 1], accum_out=den[:, m, h:h + 1])
                    last = nc.scalar.activation(probs[:, i % 2, SEQ:NC], B(("s", i))[:, SEQ:NC], ACT.Exp,
                                                bias=neg_max[:, 2 * i + 1:2 * i + 2],
                                                accum_out=den[:, m, h + 1:h + 2])
                else:
                    m, s = (i - 8) // 4, i % 4
                    last = nc.scalar.activation(probs[:, i % 2, :], B(("s", i))[:, :], ACT.Exp,
                                                bias=neg_max[:, 2 * i:2 * i + 1],
                                                accum_out=den[:, m, 8 + s:9 + s])
                free(last, ("s", i))

            def x_squares(lay, m, half):
                room = (probs, probsT)[half][:, m, :]
                nc.scalar.activation(room, x_sb[:, m, NC * half:NC * half + NC], ACT.Square,
                                     accum_out=ssx[:, half, m:m + 1]).then_inc(x_sums, 1)

            act.wait_ge(half_ready, 1)
            nc.scalar.activation(table_warm[:, :], neg_half[:, 0, 0:MT], ACT.Exp)
            act.wait_ge(x0_loaded, 16)
            for i in range(EARLY_TURNS):
                turn(BEFORE, ("mix_x", i))
            with act.Fori(0, DEPTH) as lay:
                for t in range(UNITS):
                    for name in turns_before(t):
                        turn(lay, name)
                    if t == 0:
                        split_first(lay)
                    for j in splits_at(t, ahead=3):
                        split(lay, j)
                    if 0 <= t - ATT_STEP < ATT:
                        softmax_exp(lay, t - ATT_STEP)
                    if t in (25, 26):
                        n = t - 25
                        for m in range(MT):
                            wait_emptied(act, lay, (f"z{Z_CHUNKS - 2 + n}", m))
                            nc.scalar.activation(gate_v3[:, m, :, n, :], gate_v3[:, m, :, n, :],
                                                 ACT.Sigmoid).then_inc(gate_done, 1)
                    for name in turns_within(t):
                        turn(lay, name)
                    if t == 0:
                        for half in range(2):
                            for m in range(MT):
                                b = X_BANKS[half] + m
                                act.wait_ge(bank_free[b], lay * USES[b] + 1)
                                if half == 1:
                                    act.wait_ge(x1_loaded, 16)
                                x_squares(lay, m, half)
                    if t % 2 == 1 and t // 2 <= POOL_CHUNK:
                        c = t // 2
                        if c == 0:
                            act.wait_ge(x_norm, lay * 2 + 1)
                        if c == 4:
                            act.wait_ge(mask_ready, 2)
                        for m in range(MT):
                            wait_full(act, lay, (f"z{c}", m))
                            for off, w, to, at in Z_PIECES[c]:
                                dst = (zqk if to == "qk" else zvu)[:, m, at:at + w]
                                src = B((f"z{c}", m))[:, off:off + w]
                                if c == 0:
                                    dst = dst.rearrange("p (j g d) -> p g j d", g=2, d=HD)
                                    src = src.rearrange("p (g j d) -> p g j d", g=2, d=HD)
                                if to == "qk":
                                    square = squares[:, m, at:at + w]
                                    if c == 0:
                                        square = square.rearrange("p (j g d) -> p g j d", g=2, d=HD)
                                    nc.scalar.activation(square, src, ACT.Square, scale=rstd[:, 0, m:m + 1])
                                last = nc.scalar.activation(dst, src, ACT.Copy,
                                                            scale=rstd[:, 0, m:m + 1])
                            free(last, (f"z{c}", m))
                    if t in (U_OUT + 3, U_FFN):
                        half = t - U_OUT - 3
                        for m in range(MT):
                            wait_emptied(act, lay, (f"W{half}", m))
                            x_squares(lay, m, half)
                    i, odd = divmod(t - U_FFN, 2)
                    if 0 <= i < FC and odd:
                        if i == 0:
                            act.wait_ge(x_norm, lay * 2 + 2)
                        for m in range(MT):
                            wait_full(act, lay, (f"f{i}", m))
                            nc.scalar.activation(sg[:, i % 2, m, :], B((f"f{i}", m))[:, 0:256], ACT.Sigmoid,
                                                 scale=rstd[:, 1, m:m + 1]).then_inc(sig_done, 1)

        @block.vector
        def _(dve):
            links = [0]

            def link(ins):
                links[0] += 1
                ins.then_inc(vchain, 1)
                return links[0]

            def after(lay, n):
                dve.wait_ge(vchain, lay * VECTOR_LINKS + n)

            def split(lay, j):
                dve.wait_ge(unit_hi, lay * (UNITS - 1) + j)
                w = [a[:, j % RING, :, :].rearrange("p k n -> p (k n)") for a in (w_lo, w_raw, w_hi)]
                nc.vector.tensor_tensor(w[0], w[1], w[2].bitcast(F32), ALU.subtract).then_inc(unit_lo, 1)

            def split_first(lay):
                for k in range(UK):
                    dve.wait_ge(first_hi, lay * UK + (k + 1))
                    nc.vector.tensor_tensor(w_lo[:, 0, k, :], w_raw[:, 0, k, :], w_hi[:, 0, k, :].bitcast(F32),
                                            ALU.subtract).then_inc(first_lo, 1)

            def scale_turn(lay, name):
                kind, i = name
                n = SCALED_TURNS.index(name)
                wait_full(dve, lay, name)
                if lay is not BEFORE:
                    dve.wait_ge(turn_lo, lay * len(SCALED_TURNS) + (n + EARLY_TURNS - 1))
                if kind == "mixed":
                    gain = par[:, PR_PS + 2 * i:PR_PS + 2 * i + 2].unsqueeze(2).to_broadcast([P, 2, SEQ])
                else:
                    first = (PR_MIX if kind == "mix_x" else PR_FFN) + UK * (i // 2)
                    gain = par[:, first:first + UK].unsqueeze(2).to_broadcast([P, UK, P])
                src = turn_view(name, B(name)[:, :])
                dst = turn_view(name, scratch[:, NC * (n % 2):NC * (n % 2) + NC])
                free(nc.vector.tensor_tensor(dst, src, gain, ALU.mult), name)

            def low_turn(lay, name):
                n = HI_TURNS.index(name)
                dve.wait_ge(turn_hi, lay * len(HI_TURNS) + (n + 1 + EARLY_TURNS))
                hi = turn_dest(name, True).bitcast(F32)
                if name[0] in SCALED:
                    k = SCALED_TURNS.index(name)
                    src = scratch[:, NC * (k % 2):NC * (k % 2) + NC]
                    nc.vector.tensor_tensor(turn_dest(name, False), turn_view(name, src), hi, ALU.subtract
                                            ).then_inc(turn_lo, 1)
                else:
                    ins = nc.vector.tensor_tensor(turn_dest(name, False), turn_view(name, B(name)[:, :]), hi,
                                                  ALU.subtract)
                    free(ins, name)

            def turns(lay, names):
                names = [n for n in names if n[0] in SCALED + SPLIT]
                for name in names:
                    if name[0] in SCALED:
                        scale_turn(lay, name)
                for name in names:
                    low_turn(lay, name)

            def rope_tables(lay):
                for k in range(4):
                    axial = k < 2
                    cos, sin = rope_c[:, 0 if axial else 2, :, :], rope_c[:, 1 if axial else 3, :, :]
                    g = par[:, PR_GAIN + HD * k:PR_GAIN + HD * (k + 1)]
                    link(nc.vector.tensor_tensor(rope[:, k, 0, :, :], cos,
                                                 g.unsqueeze(1).to_broadcast([P, MT, HD]), ALU.mult))
                    r = 2 if axial else 1
                    w = HD // (2 * r)
                    for half in range(2):
                        o = rope[:, k, 1, :, :].rearrange("p m (r h w) -> p m r h w", r=r, h=2)[:, :, :, half, :]
                        s = sin.rearrange("p m (r h w) -> p m r h w", r=r, h=2)[:, :, :, half, :]
                        gp = g.rearrange("p (r h w) -> p r h w", r=r, h=2)[:, :, 1 - half, :]
                        link(nc.vector.tensor_tensor(o, s, gp.unsqueeze(1).to_broadcast([P, MT, r, w]), ALU.mult))
                return links[0]

            def rotate(lay, n, region, m, tables):
                _, col, hs, first, k, chunk, _ = region
                W = hs * HD
                z = zqk[:, m, col:col + W]
                t2 = scratch[:, 0:W]
                wait_emptied(dve, lay, (f"z{chunk}", m))
                nc.vector.tensor_reduce(ss[:, m, first:first + hs],
                                        squares[:, m, col:col + W].rearrange("p (h d) -> p h d", d=HD), AX_X,
                                        ALU.add).then_inc(head_sums, 1)
                if n:
                    after(lay, turned_by[n - 1])
                else:
                    wait_lo(dve, lay, ("mix_x", 3))
                r = 2 if k < 2 else 1
                w = HD // (2 * r)
                after(lay, tables)
                for half in range(2):
                    def part(a, h):
                        return a.rearrange("p (q r h w) -> p q r h w", r=r, h=2, w=w)[:, :, :, h, :]
                    table = rope[:, k, 1, m, :].rearrange("p (r h w) -> p r h w", r=r, h=2)[:, :, half, :]
                    partner = nc.vector.tensor_tensor(part(t2, half), part(z, 1 - half),
                                                      table.unsqueeze(1).to_broadcast([P, hs, r, w]), ALU.mult)
                partner = link(partner)
                after(lay, partner)
                c = link(nc.vector.tensor_tensor(z.rearrange("p (h d) -> p h d", d=HD),
                                                 z.rearrange("p (h d) -> p h d", d=HD),
                                                 rope[:, k, 0, m, :].unsqueeze(1).to_broadcast([P, hs, HD]),
                                                 ALU.mult))
                after(lay, c)
                turned_by.append(link(nc.vector.tensor_tensor(z, z, t2, ALU.add)))

            def norm_rotated(lay, n, region, m):
                _, col, hs, first = region[:4]
                z = zqk[:, m, col:col + hs * HD].rearrange("p (h d) -> p h d", d=HD)
                after(lay, turned_by[n])
                dve.wait_ge(head_norms, lay * TURNED + (n + 1))
                nc.vector.tensor_tensor(z, z, rs[:, m, first:first + hs].unsqueeze(2).to_broadcast([P, hs, HD]),
                                        ALU.mult).then_inc(rotated, 1)

            def row_max(lay, i):
                wait_full(dve, lay, ("s", i))
                k = 2 if i < 8 else 1
                nc.vector.tensor_reduce(neg_max[:, 2 * i:2 * i + k],
                                        B(("s", i))[:, :].rearrange("p (h n) -> p h n", h=k), AX_X, ALU.max,
                                        negate=True).then_inc(max_ready, 1)

            def norm_heads(lay, o):
                m, h0, hs = o % 2, (0 if o < 2 else 8), (8 if o < 2 else SLOTS)
                wait_full(dve, lay, ("o", o))
                r = link(nc.vector.reciprocal(rden[:, m, h0:h0 + hs], den[:, m, h0:h0 + hs]))
                after(lay, r)
                free(nc.vector.tensor_tensor(
                    heads[:, m, h0 * HD:(h0 + hs) * HD].rearrange("p (h d) -> p h d", d=HD),
                    B(("o", o))[:, 0:hs * HD].rearrange("p (h d) -> p h d", d=HD),
                    rden[:, m, h0:h0 + hs].unsqueeze(2).to_broadcast([P, hs, HD]), ALU.mult), ("o", o))

            def merge(lay, branch, n, written, scratch_read):
                names = [("ABC"[branch] + str(n), m) for m in range(MT)]
                for m in range(MT):
                    wait_full(dve, lay, names[m])
                    if branch == 2:
                        dve.wait_ge(gate_done, lay * 4 + (2 * n + m + 1))
                        to = merged[:, m, NC * n:NC * n + NC]
                    else:
                        if scratch_read[m]:
                            dve.wait_ge(*scratch_read[m])
                        to = scratch[:, NC * m:NC * m + NC]
                    gate = gates[:, m, D * branch + NC * n:D * branch + NC * n + NC]
                    free(nc.vector.tensor_tensor(to, B(names[m])[:, :], gate, ALU.mult), names[m])
                if branch == 2:
                    return
                for m in range(MT):
                    wait_emptied(dve, lay, names[m])
                    if written[n][m] is None:
                        wait_emptied(dve, lay, (f"C{n}", m))
                    else:
                        after(lay, written[n][m])
                    to = merged[:, m, NC * n:NC * n + NC]
                    ins = nc.vector.tensor_tensor(to, to, scratch[:, NC * m:NC * m + NC], ALU.add)
                    if written[n][m] is None:
                        written[n][m] = link(ins)
                        scratch_read[m] = (vchain, lay * VECTOR_LINKS + written[n][m])
                    else:
                        ins.then_inc(merged_ready, 1)
                        scratch_read[m] = (merged_ready, lay * 4 + (2 * n + m + 1))

            def add_x(lay, name, n):
                for m in range(MT):
                    wait_full(dve, lay, (name, m))
                    part = x_sb[:, m, NC * n:NC * n + NC]
                    free(nc.vector.tensor_tensor(part, B((name, m))[:, :], part, ALU.add), (name, m))

            dve.wait_ge(gains_loaded, 16)
            turns(BEFORE, [("mix_x", i) for i in range(EARLY_TURNS)])
            with dve.Fori(0, DEPTH) as lay:
                links[0] = 0
                written, scratch_read = [[None] * MT, [None] * MT], [None] * MT
                turned_by = []
                for t in range(UNITS):
                    if 0 <= t - ATT_STEP < ATT:
                        row_max(lay, t - ATT_STEP)
                    if t in (15, 19, 23, 27):
                        norm_heads(lay, (t - 15) // 4)
                    if t == U_DOWN + 7:
                        dve.wait_ge(gains_loaded, lay * 16 + 32)
                    turns(lay, turns_before(t))
                    if t == 0:
                        split_first(lay)
                    if t in TURNS_FIRST:
                        turns(lay, turns_within(t))
                    for j in splits_at(t):
                        split(lay, j)
                    if t not in TURNS_FIRST:
                        turns(lay, turns_within(t))
                    if t == 1:
                        dve.wait_ge(angles_loaded, 16)
                        dve.wait_ge(params_loaded, lay * 16 + 16)
                        tables = rope_tables(lay)
                    for r, region in enumerate(REGIONS):
                        for m in range(MT):
                            if region[-1][m] == t - 1:
                                norm_rotated(lay, 2 * r + m, region, m)
                    for r, region in enumerate(REGIONS):
                        for m in range(MT):
                            if region[-1][m] == t:
                                rotate(lay, 2 * r + m, region, m, tables)
                    c, odd = divmod(t, 2)
                    if odd and GATE_CHUNK <= c < Z_CHUNKS:
                        g = c - GATE_CHUNK
                        if g == 0:
                            dve.wait_ge(head_sums, lay * TURNED + TURNED)
                        dve.wait_ge(bias_loaded[g % 2], lay * 48 + 16 * (g // 2 + 1))
                        for m in range(MT):
                            wait_full(dve, lay, (f"z{c}", m))
                            free(nc.vector.scalar_tensor_tensor(
                                gates[:, m, NC * g:NC * g + NC], B((f"z{c}", m))[:, :], rstd[:, 0, m:m + 1],
                                bias_sb[:, g % 2, :], ALU.mult, ALU.add), (f"z{c}", m))
                    for unit, branch, n in ((U_C0, 2, 0), (U_C1, 2, 1), (U_A0, 0, 0), (U_B, 1, 0), (U_B, 1, 1),
                                            (U_A1, 0, 1)):
                        if t == unit:
                            merge(lay, branch, n, written, scratch_read)
                    if t == U_OUT + 2:
                        add_x(lay, "W0", 0)
                    if t == U_OUT + 3:
                        add_x(lay, "W1", 1)
                    i, odd = divmod(t - U_FFN, 2)
                    if 0 <= i < FC and odd:
                        made = []
                        for m in range(MT):
                            dve.wait_ge(sig_done, lay * 2 * FC + (2 * i + m + 1))
                            made.append(link(nc.vector.scalar_tensor_tensor(
                                scratch[:, 2 * NC + 256 * m:2 * NC + 256 * m + 256], B((f"f{i}", m))[:, 0:256],
                                rstd[:, 1, m:m + 1], sg[:, i % 2, m, :], ALU.mult, ALU.mult)))
                        for m in range(MT):
                            after(lay, made[m])
                            free(nc.vector.scalar_tensor_tensor(
                                hid[:, i % 2, m, :], B((f"f{i}", m))[:, 256:NC], rstd[:, 1, m:m + 1],
                                scratch[:, 2 * NC + 256 * m:2 * NC + 256 * m + 256], ALU.mult, ALU.mult),
                                (f"f{i}", m))
                    if t == U_DOWN + 5:
                        add_x(lay, "D0", 0)
                    if t == U_DOWN + 10:
                        add_x(lay, "D1", 1)
                assert links[0] == VECTOR_LINKS, links[0]

        @block.tensor
        def _(pe):
            pe.sem_inc(unit_done, RING)

            def rows(lay, t, name, m, src, tiles, wk, first, final, opening=False):
                tok = slice(P * m, P * m + P)
                o, slot = B((name, m))[:, :], t % RING
                if first:
                    wait_free(pe, lay, (name, m))
                if opening and t:
                    pe.wait_ge(unit_hi, lay * (UNITS - 1) + t)
                for i, k in enumerate(tiles):
                    if opening and not t:
                        pe.wait_ge(first_hi, lay * UK + (i + 1))
                    nc.tensor.matmul(o, src[0][:, k, tok], w_hi[:, slot, wk + i, :], start=first and i == 0,
                                     stop=False)
                    nc.tensor.matmul(o, src[1][:, k, tok], w_hi[:, slot, wk + i, :], start=False, stop=False)
                if opening and t in TURNS_FIRST:
                    for turn in turns_within(t):
                        transposes(lay, turn)
                if opening and t:
                    pe.wait_ge(unit_lo, lay * (UNITS - 1) + t)
                for i, k in enumerate(tiles):
                    if opening and not t:
                        pe.wait_ge(first_lo, lay * UK + (i + 1))
                    last = nc.tensor.matmul(o, src[0][:, k, tok], w_lo[:, slot, wk + i, :], start=False,
                                            stop=final and i == len(tiles) - 1)
                if final:
                    full(last, (name, m))
                return last

            def columns(lay, t, name, src, tiles, first, final, wk=0):
                rows(lay, t, name, 0, src, tiles, wk, first, final, opening=wk == 0)
                if wk == 0 and t not in TURNS_FIRST:
                    for turn in turns_within(t):
                        transposes(lay, turn)
                return rows(lay, t, name, 1, src, tiles, wk, first, final)

            def transposes(lay, name):
                kind, i = name
                b = B(name)
                wait_free(pe, lay, name)

                def turn(at, src):
                    return nc.tensor.transpose(b[:, at:at + P], src, ident[:, :])

                if kind in ("mix_x", "ffn_x"):
                    half, m = divmod(i, 2)
                    if kind == "mix_x" and half == 0:
                        if lay is not BEFORE:
                            wait_emptied(pe, lay, ("D0", m))
                    elif kind == "mix_x":
                        done = X_BANKS[1] + m
                        pe.wait_ge(bank_free[done], lay * USES[done] + 1)
                        pe.wait_ge(x1_loaded, 16)
                    else:
                        wait_emptied(pe, lay, (f"W{half}", m))
                    for k in range(UK):
                        last = turn(P * k, x_sb[:, m, P * (UK * half + k):P * (UK * half + k + 1)])
                elif kind == "merged":
                    half, m = divmod(i, 2)
                    pe.wait_ge(merged_ready, lay * 4 + (i + 1))
                    for k in range(UK):
                        last = turn(P * k, merged[:, m, P * (UK * half + k):P * (UK * half + k + 1)])
                elif kind == "qk":
                    first, k = QK_BATCH[i]
                    region = (0, 0, 1, 2, 3, 3, 4, 4, 5)[i]
                    pe.wait_ge(rotated, lay * TURNED + 2 * (region + 1))
                    for j in range(k):
                        for m in range(MT):
                            last = turn(P * (2 * j + m), zqk[:, m, P * (first + j):P * (first + j + 1)])
                elif kind == "probs":
                    wait_emptied(pe, lay, ("s", i))
                    for c in range(4):
                        last = turn(P * c, probs[:, i % 2, P * c:P * c + P])
                elif kind == "heads":
                    wait_emptied(pe, lay, ("o", i))
                    m, c0, k = i % 2, (0 if i < 2 else A_Q), (4 if i < 2 else 2)
                    for c in range(k):
                        last = turn(P * c, heads[:, m, c0 + P * c:c0 + P * c + P])
                elif kind == "hidden":
                    for m in range(MT):
                        wait_emptied(pe, lay, (f"f{i}", m))
                    for k in range(2):
                        for m in range(MT):
                            last = turn(P * (2 * k + m), hid[:, i % 2, m, P * k:P * k + P])
                elif kind == "pool":
                    if i == 0:
                        pe.wait_ge(pooling_loaded, 16)
                        for m in range(MT):
                            wait_emptied(pe, lay, (f"z{POOL_CHUNK}", m))
                    for g in (2 * i, 2 * i + 1):
                        for m in range(MT):
                            last = nc.tensor.matmul(b[:, SEQ * (g % 2):SEQ * (g % 2) + SEQ],
                                                    zvu[:, m, VU_POOL + P * g:VU_POOL + P * g + P],
                                                    pool_mat[:, m, g, :], start=(m == 0), stop=(m == MT - 1))
                else:
                    wait_emptied(pe, lay, ("pool", i))
                    for g in (2 * i, 2 * i + 1):
                        last = nc.tensor.matmul(b[:, SEQ * (g % 2):SEQ * (g % 2) + SEQ], lin[:, g, :],
                                                pooledT[:, g, :], start=True, stop=True)
                full(last, name)

            def scores(lay, i):
                wait_free(pe, lay, ("s", i))
                b = B(("s", i))
                if i == 0:
                    wait_emptied(pe, lay, ("qk", 2))
                if i == 8:
                    pe.wait_ge(mask_ready, 2)
                    wait_emptied(pe, lay, ("qk", 7))
                    wait_emptied(pe, lay, ("qk", 8))
                if i < 8:
                    m, (g, pair) = i // 4, divmod(i % 4, 2)
                    part = slice(HD * g, HD * g + HD)
                    for hh in range(2):
                        last = nc.tensor.matmul(b[:, SEQ * hh:SEQ * hh + SEQ],
                                                qkT[part, QT_A_Q + 2 * pair + hh, P * m:P * m + P],
                                                qkT[part, QT_A_K, :], start=True, stop=True)
                else:
                    m, s = (i - 8) // 4, i % 4
                    nc.tensor.matmul(b[:, :], ident_b, mask_m[m], start=True, stop=False)
                    part = slice(HD * (s % 2), HD * (s % 2) + HD)
                    for g in range(GROUPS):
                        tile = 2 * g + s // 2
                        cols, keys = (slice(0, SEQ), slice(0, SEQ)) if g == 0 else \
                            (slice(SEQ + P * (g - 1), SEQ + P * g), slice(P * m, P * m + P))
                        last = nc.tensor.matmul(b[:, cols], qkT[part, QT_B_Q + tile, P * m:P * m + P],
                                                qkT[part, QT_B_K + tile, keys], start=False,
                                                stop=(g == GROUPS - 1))
                full(last, ("s", i))

            def values(lay, i):
                wait_emptied(pe, lay, ("probs", i))
                if i < 8:
                    m, h, o = i // 4, 2 * (i % 4), i // 4
                    todo = [(h + hh, [(2 * hh + kt, kt, VU_A + HD * ((h + hh) // 4)) for kt in range(MT)])
                            for hh in range(2)]
                else:
                    m, s, o = (i - 8) // 4, i % 4, 2 + (i - 8) // 4
                    v = [VU_B + HD * (SLOTS * g + s) for g in range(GROUPS)]
                    todo = [(s, [(0, 0, v[0]), (1, 1, v[0]), (2, m, v[1]), (3, m, v[2])])]
                if i % 4 == 0:
                    wait_free(pe, lay, ("o", o))
                for h, terms in todo:
                    for n, (c, kt, col) in enumerate(terms):
                        last = nc.tensor.matmul(B(("o", o))[:, HD * h:HD * h + HD],
                                                probsT[:, i % 2, P * c:P * c + P], zvu[:, kt, col:col + HD],
                                                start=(n == 0), stop=(n == len(terms) - 1))
                if i % 4 == 3:
                    full(last, ("o", o))

            aT, oT, mixT, hT = (aT_hi, aT_lo), (oT_hi, oT_lo), (mixT_hi, mixT_lo), (hT_hi, hT_lo)
            pe.wait_ge(x0_loaded, 16)
            pe.wait_ge(eye_loaded, 16)
            for i in range(EARLY_TURNS):
                transposes(BEFORE, ("mix_x", i))
            with pe.Fori(0, DEPTH) as lay:
                for t in range(UNITS):
                    for name in turns_before(t):
                        if name[0] == "probs":
                            transposes(lay, name)
                    if 0 <= t - ATT_STEP < ATT:
                        scores(lay, t - ATT_STEP)
                    if 0 <= t - ATT_STEP - 3 < ATT:
                        values(lay, t - ATT_STEP - 3)
                    for name in turns_before(t):
                        if name[0] != "probs":
                            transposes(lay, name)
                    if t < U_C0:
                        c, half = divmod(t, 2)
                        if c == 0:
                            for m in range(MT):
                                wait_lo(pe, lay, ("mix_x", 2 * half + m), former=half == 0)
                        last = columns(lay, t, f"z{c}", aT, range(UK * half, UK * half + UK), half == 0, half == 1)
                    elif t in (U_C0, U_C1):
                        if t == U_C0:
                            for i in range(2):
                                wait_lo(pe, lay, ("mixed", i))
                        last = columns(lay, t, f"C{t - U_C0}", mixT, range(4), True, True)
                    elif t in (U_A0, U_A1):
                        if t == U_A0:
                            wait_emptied(pe, lay, ("heads", 0))
                            wait_emptied(pe, lay, ("heads", 1))
                        last = columns(lay, t, "A0" if t == U_A0 else "A1", oT, range(4), True, True)
                    elif t == U_B:
                        wait_emptied(pe, lay, ("heads", 2))
                        wait_emptied(pe, lay, ("heads", 3))
                        columns(lay, t, "B0", oT, (4, 5), True, True)
                        last = columns(lay, t, "B1", oT, (4, 5), True, True, wk=2)
                    elif t < U_FFN:
                        half, n = divmod(t - U_OUT, 2)
                        if n == 0:
                            for m in range(MT):
                                wait_emptied(pe, lay, ("merged", 2 * half + m))
                        last = columns(lay, t, f"W{n}", aT, range(UK * half, UK * half + UK), half == 0, half == 1)
                    elif t < U_DOWN:
                        i, half = divmod(t - U_FFN, 2)
                        if i == 0:
                            for m in range(MT):
                                wait_lo(pe, lay, ("ffn_x", 2 * half + m))
                        last = columns(lay, t, f"f{i}", aT, range(UK * half, UK * half + UK), half == 0, half == 1)
                    else:
                        q = t - U_DOWN
                        if q < 5:
                            for i in (2 * q, 2 * q + 1):
                                wait_emptied(pe, lay, ("hidden", i))
                            last = columns(lay, t, "D0", hT, range(UK * q, UK * q + UK), q == 0, False)
                        elif q == 5:
                            wait_emptied(pe, lay, ("hidden", FC - 1))
                            columns(lay, t, "D0", hT, (20, 21), False, True)
                            last = columns(lay, t, "D1", hT, (20, 21), True, False, wk=2)
                        else:
                            q -= 6
                            last = columns(lay, t, "D1", hT, range(UK * q, UK * q + UK), False, q == 4)
                    last.then_inc(unit_done, 1)


def constants():
    import numpy as np
    tok = np.stack([2 * np.arange(P) + m for m in range(MT)])
    flat = tok.reshape(-1)

    def angles(pos, dim):
        inv = np.float32(10000.0) ** (-np.arange(0, dim, 2, dtype=np.float32) / np.float32(dim))
        return (pos.astype(np.float32)[..., None] * inv.astype(np.float32)).astype(np.float32)

    def table(parts):
        cos = np.concatenate([np.concatenate([np.cos(a), np.cos(a)], -1) for a in parts], -1)
        sin = np.concatenate([np.concatenate([-np.sin(a), np.sin(a)], -1) for a in parts], -1)
        return cos, sin

    axial = table([angles(tok // 64, HD // 2), angles(tok % 64, HD // 2)])
    plain = table([angles(tok, HD)])
    rope = np.stack([axial[0], axial[1], plain[0], plain[1]])
    pool = np.zeros((SEQ, POOL_G, SEQ), np.float32)
    for g, w in enumerate((2, 4, 8, 16)):
        for n, t in enumerate(flat):
            lo, hi = max(t - w // 2, 0), min(t + w - w // 2, SEQ)
            inside = (flat >= lo) & (flat < hi)
            pool[inside, g, n] = np.float32(1.0) / np.float32(hi - lo)
            pool[n, g, n] -= np.float32(1.0)
    eye = np.eye(P, dtype=np.float32)
    rope = np.ascontiguousarray(rope.transpose(2, 0, 1, 3).reshape(P, -1), np.float32)
    pool = np.ascontiguousarray(pool.reshape(MT, P, POOL_G, SEQ).transpose(1, 0, 2, 3).reshape(P, -1))
    masks = []
    for m in range(MT):
        q = tok[m][:, None]
        masks.append(np.concatenate([
            np.where(np.abs(q - flat[None, :]) <= 64, 0.0, NEG_INF),
            np.where((q - tok[m][None, :]) % 4 == 0, 0.0, NEG_INF),
            np.where((q - tok[m][None, :]) % 16 == 0, 0.0, NEG_INF)], 1))
    return {"eye": eye, "angles": rope, "pooling": pool, "mask": np.concatenate(masks, 1).astype(np.float32)}


def weight_stream(w_in, w_branch_a, w_branch_b, w_branch_c, w_out, w_ffn_gate, w_ffn_up, w_ffn_down):
    import numpy as np
    units = np.empty((DEPTH, UNITS, P, UK, NC), np.float32)
    for l in range(DEPTH):
        u = units[l]
        w = w_in[l].reshape(2, UK, P, Z_CHUNKS, NC)
        u[:U_C0] = w.transpose(3, 0, 2, 1, 4).reshape(2 * Z_CHUNKS, P, UK, NC)
        c = w_branch_c[l].reshape(UK, P, 2, NC)
        a = w_branch_a[l].reshape(UK, P, 2, NC)
        for n, (uc, ua) in enumerate(((U_C0, U_A0), (U_C1, U_A1))):
            u[uc] = c[:, :, n].transpose(1, 0, 2)
            u[ua] = a[:, :, n].transpose(1, 0, 2)
        b = w_branch_b[l].reshape(2, P, 2, NC)
        u[U_B] = b.transpose(1, 2, 0, 3).reshape(P, UK, NC)
        w = w_out[l].reshape(2, UK, P, 2, NC)
        u[U_OUT:U_FFN] = w.transpose(0, 3, 2, 1, 4).reshape(4, P, UK, NC)
        for at, w in ((0, w_ffn_gate[l]), (256, w_ffn_up[l])):
            w = w.reshape(2, UK, P, FC, 256).transpose(3, 0, 2, 1, 4)
            u[U_FFN:U_DOWN, :, :, at:at + 256] = w.reshape(2 * FC, P, UK, 256)
        w = w_ffn_down[l].reshape(KF, P, 2, NC)
        for n, first in ((0, U_DOWN), (1, U_DOWN + 6)):
            u[first:first + 5] = w[:20, :, n].reshape(5, UK, P, NC).transpose(0, 2, 1, 3)
        u[U_DOWN + 5] = w[20:].transpose(1, 2, 0, 3).reshape(P, UK, NC)
    return units.reshape(DEPTH * UNITS, P, UNIT)


def layer_params(norm_mix, norm_ffn, pool_scale, qn_a, kn_a, qn_b, kn_b, pool_lin):
    import numpy as np
    par = np.empty((DEPTH, P, PR_W), np.float32)
    par[:, :, PR_MIX:PR_MIX + KT] = norm_mix.reshape(DEPTH, KT, P).transpose(0, 2, 1)
    par[:, :, PR_FFN:PR_FFN + KT] = norm_ffn.reshape(DEPTH, KT, P).transpose(0, 2, 1)
    par[:, :, PR_PS:PR_PS + POOL_G] = pool_scale.reshape(DEPTH, POOL_G, P).transpose(0, 2, 1)
    for k, g in enumerate((qn_a, kn_a, qn_b, kn_b)):
        par[:, :, PR_GAIN + HD * k:PR_GAIN + HD * (k + 1)] = g[:, None, :]
    par[:, :, PR_LIN:] = pool_lin.transpose(0, 2, 1, 3).reshape(DEPTH, P, POOL_G * P)
    return par


def kernel(**inputs):
    import numpy as np
    import concourse.bacc as bacc
    from concourse.bass_utils import run_bass_kernel_spmd

    i = {k: np.asarray(v) for k, v in inputs.items()}
    host = {
        "x": np.ascontiguousarray(i["x"]),
        "stream": weight_stream(i["w_in"], i["w_branch_a"], i["w_branch_b"], i["w_branch_c"], i["w_out"],
                                i["w_ffn_gate"], i["w_ffn_up"], i["w_ffn_down"]),
        "params": layer_params(i["norm_mix"], i["norm_ffn"], i["pool_scale"], i["qn_a"], i["kn_a"], i["qn_b"],
                               i["kn_b"], i["pool_lin"]),
        "b_gate": np.ascontiguousarray(i["b_gate"].reshape(DEPTH, 3 * D // NC, NC)),
        **constants(),
    }
    nc = bacc.Bacc("TRN2", target_bir_lowering=False, num_devices=1, dynamic_dma_scratch_size=4096)
    arrays, args = {}, []
    for name, a in host.items():
        arrays[f"in_{name}_dram"] = a
        args.append(nc.dram_tensor(f"in_{name}_dram", a.shape, mybir.dt.from_np(a.dtype), kind="ExternalInput").ap())
    args.append(nc.dram_tensor("out_0_dram", (1, SEQ, D), F32, kind="ExternalOutput").ap())
    build(nc, *args)
    r = run_bass_kernel_spmd(nc, [arrays], core_ids=[0])
    return r.results[0]["out_0_dram"]
```
